# Optimizing a Trainium2 kernel written in Bass

```python
import math
import jax, jax.numpy as jnp
from jax import lax
import numpy as np

D_MODEL = 1024
BATCH = 1
SEQ = 256
DEPTH = 2

CHUNK = 64
D_CONV = 1024
CONV_GROUPS = 16
CONV_WIDTH = 3
D_SSM = 512
SSM_GROUP = 16
N_SSM_GROUPS = D_SSM // SSM_GROUP
SSM_STATE = 64
N_BRANCH = 2
PROJ_WIDTH = 3 * D_CONV + D_SSM + N_BRANCH * D_MODEL
D_FF = 7 * D_MODEL // 2
N_EXPERTS = 8
TOP_K = 2
N_DENSE = (DEPTH + 1) // 2
N_MOE = DEPTH // 2
RMS_EPS = 1e-6
DT_MIN = 1e-3
DT_MAX = 1e-1

kernel_name = "hybrid_conv_s5_moe_encoder"

def rmsnorm(x, g):
    xf = x.astype(jnp.float32)
    y = xf * lax.rsqrt(jnp.mean(xf * xf, axis=-1, keepdims=True) + RMS_EPS)
    return (y * g.astype(jnp.float32)).astype(x.dtype)

def short_conv_branch(b_gate, c_gate, v, conv_w, w_out):
    u = c_gate * v
    rhs = conv_w.reshape(CONV_WIDTH, 1, D_CONV).astype(u.dtype)
    conv = lax.conv_general_dilated(
        u, rhs, window_strides=(1,), padding=[(CONV_WIDTH - 1, 0)],
        dimension_numbers=("NWC", "WIO", "NWC"), feature_group_count=D_CONV)
    return (b_gate * conv) @ w_out

def _ssm_combine(e_i, e_j):
    ar_i, ai_i, br_i, bi_i = e_i
    ar_j, ai_j, br_j, bi_j = e_j
    return (ar_j * ar_i - ai_j * ai_i,
            ar_j * ai_i + ai_j * ar_i,
            ar_j * br_i - ai_j * bi_i + br_j,
            ar_j * bi_i + ai_j * br_i + bi_j)

def s5_branch(u, a_re, a_im, log_dt, b_re, b_im, c_re, c_im, d_skip, w_glu):
    bsz, seq, _ = u.shape
    f32 = jnp.float32
    uf = u.astype(f32).reshape(bsz, seq, N_SSM_GROUPS, SSM_GROUP)
    ar = a_re.astype(f32)
    ai = a_im.astype(f32)
    dt = jnp.exp(log_dt.astype(f32))[:, None]
    mag = jnp.exp(ar * dt)
    abar_re = mag * jnp.cos(ai * dt)
    abar_im = mag * jnp.sin(ai * dt)
    den = ar * ar + ai * ai
    nr = abar_re - 1.0
    ni = abar_im
    coef_re = (nr * ar + ni * ai) / den
    coef_im = (ni * ar - nr * ai) / den
    br = b_re.astype(f32)
    bi = b_im.astype(f32)
    bb_re = coef_re[..., None] * br - coef_im[..., None] * bi
    bb_im = coef_re[..., None] * bi + coef_im[..., None] * br
    bu_re = jnp.einsum("blgc,gnc->lbgn", uf, bb_re)
    bu_im = jnp.einsum("blgc,gnc->lbgn", uf, bb_im)
    a_seq_re = jnp.broadcast_to(abar_re, (seq, 1, N_SSM_GROUPS, SSM_STATE))
    a_seq_im = jnp.broadcast_to(abar_im, (seq, 1, N_SSM_GROUPS, SSM_STATE))
    _, _, s_re, s_im = lax.associative_scan(
        _ssm_combine, (a_seq_re, a_seq_im, bu_re, bu_im), axis=0)
    y = (jnp.einsum("gcn,lbgn->blgc", c_re.astype(f32), s_re)
         - jnp.einsum("gcn,lbgn->blgc", c_im.astype(f32), s_im))
    y = y.reshape(bsz, seq, D_SSM) + d_skip.astype(f32) * u.astype(f32)
    y = jax.nn.gelu(y).astype(u.dtype)
    z = y @ w_glu
    return z[..., :D_MODEL] * jax.nn.sigmoid(z[..., D_MODEL:])

def swiglu(h, w_gate, w_up, w_down):
    return (jax.nn.silu(h @ w_gate) * (h @ w_up)) @ w_down

def moe_swiglu(h, router_w, router_b, w_gate, w_up, w_down):
    logits = (h @ router_w).astype(jnp.float32) + router_b.astype(jnp.float32)
    top_val, top_idx = lax.top_k(logits, TOP_K)
    top_w = jax.nn.softmax(top_val, axis=-1)
    gate = jnp.sum(jax.nn.one_hot(top_idx, N_EXPERTS, dtype=jnp.float32) * top_w[..., None],
                   axis=-2).astype(h.dtype)
    out = jnp.zeros_like(h)
    for e in range(N_EXPERTS):
        out = out + gate[..., e:e + 1] * swiglu(h, w_gate[e], w_up[e], w_down[e])
    return out

def setup_inputs(seed: int = 0) -> dict:
    key = jax.random.key(seed)
    ks = jax.random.split(key, 32)
    f32 = jnp.float32
    nrm = lambda k, shape, scale: jax.random.normal(k, shape, f32) * scale
    n_idx = jnp.arange(SSM_STATE, dtype=f32)
    ssm_a_re = -0.5 + nrm(ks[5], (DEPTH, N_SSM_GROUPS, SSM_STATE), 0.01)
    ssm_a_im = math.pi * n_idx + nrm(ks[6], (DEPTH, N_SSM_GROUPS, SSM_STATE), 0.01)
    ssm_log_dt = jax.random.uniform(ks[7], (DEPTH, N_SSM_GROUPS), f32,
                                    math.log(DT_MIN), math.log(DT_MAX))
    return {
        "x": nrm(ks[0], (BATCH, SEQ, D_MODEL), 1.0),
        "norm_mix": 1.0 + nrm(ks[1], (DEPTH, D_MODEL), 0.02),
        "w_in": nrm(ks[2], (DEPTH, D_MODEL, PROJ_WIDTH), D_MODEL ** -0.5),
        "b_in": nrm(ks[3], (DEPTH, PROJ_WIDTH), 0.02),
        "conv_w": nrm(ks[4], (DEPTH, CONV_WIDTH, D_CONV), CONV_WIDTH ** -0.5),
        "w_conv_out": nrm(ks[8], (DEPTH, D_CONV, D_MODEL), D_CONV ** -0.5),
        "ssm_a_re": ssm_a_re,
        "ssm_a_im": ssm_a_im,
        "ssm_log_dt": ssm_log_dt,
        "ssm_b_re": nrm(ks[9], (DEPTH, N_SSM_GROUPS, SSM_STATE, SSM_GROUP), (2 * SSM_GROUP) ** -0.5),
        "ssm_b_im": nrm(ks[10], (DEPTH, N_SSM_GROUPS, SSM_STATE, SSM_GROUP), (2 * SSM_GROUP) ** -0.5),
        "ssm_c_re": nrm(ks[11], (DEPTH, N_SSM_GROUPS, SSM_GROUP, SSM_STATE), SSM_STATE ** -0.5),
        "ssm_c_im": nrm(ks[12], (DEPTH, N_SSM_GROUPS, SSM_GROUP, SSM_STATE), SSM_STATE ** -0.5),
        "ssm_d": nrm(ks[13], (DEPTH, D_SSM), 1.0),
        "w_glu": nrm(ks[14], (DEPTH, D_SSM, 2 * D_MODEL), D_SSM ** -0.5),
        "w_o": nrm(ks[15], (DEPTH, D_MODEL, D_MODEL), D_MODEL ** -0.5),
        "norm_ffn": 1.0 + nrm(ks[16], (DEPTH, D_MODEL), 0.02),
        "dense_w_gate": nrm(ks[17], (N_DENSE, D_MODEL, D_FF), D_MODEL ** -0.5),
        "dense_w_up": nrm(ks[18], (N_DENSE, D_MODEL, D_FF), D_MODEL ** -0.5),
        "dense_w_down": nrm(ks[19], (N_DENSE, D_FF, D_MODEL), D_FF ** -0.5),
        "router_w": nrm(ks[20], (N_MOE, D_MODEL, N_EXPERTS), D_MODEL ** -0.5),
        "router_b": nrm(ks[21], (N_MOE, N_EXPERTS), 0.01),
        "moe_w_gate": nrm(ks[22], (N_MOE, N_EXPERTS, D_MODEL, D_FF), D_MODEL ** -0.5),
        "moe_w_up": nrm(ks[23], (N_MOE, N_EXPERTS, D_MODEL, D_FF), D_MODEL ** -0.5),
        "moe_w_down": nrm(ks[24], (N_MOE, N_EXPERTS, D_FF, D_MODEL), D_FF ** -0.5),
        "norm_final": 1.0 + nrm(ks[25], (D_MODEL,), 0.02),
    }

def reference(x, norm_mix, w_in, b_in, conv_w, w_conv_out, ssm_a_re, ssm_a_im, ssm_log_dt,
              ssm_b_re, ssm_b_im, ssm_c_re, ssm_c_im, ssm_d, w_glu, w_o, norm_ffn,
              dense_w_gate, dense_w_up, dense_w_down, router_w, router_b,
              moe_w_gate, moe_w_up, moe_w_down, norm_final):
    o_b = 0
    o_c = o_b + D_CONV
    o_v = o_c + D_CONV
    o_u = o_v + D_CONV
    o_g = o_u + D_SSM
    for layer in range(DEPTH):
        h = rmsnorm(x, norm_mix[layer])
        proj = h @ w_in[layer] + b_in[layer]
        b_gate = proj[..., o_b:o_c]
        c_gate = proj[..., o_c:o_v]
        v = proj[..., o_v:o_u]
        u = proj[..., o_u:o_g]
        g_conv = jax.nn.sigmoid(proj[..., o_g:o_g + D_MODEL])
        g_ssm = jax.nn.sigmoid(proj[..., o_g + D_MODEL:o_g + 2 * D_MODEL])
        y_conv = short_conv_branch(b_gate, c_gate, v, conv_w[layer], w_conv_out[layer])
        y_ssm = s5_branch(u, ssm_a_re[layer], ssm_a_im[layer], ssm_log_dt[layer],
                          ssm_b_re[layer], ssm_b_im[layer], ssm_c_re[layer], ssm_c_im[layer],
                          ssm_d[layer], w_glu[layer])
        x = x + (g_conv * y_conv + g_ssm * y_ssm) @ w_o[layer]
        h = rmsnorm(x, norm_ffn[layer])
        if layer % 2 == 0:
            i = layer // 2
            f = swiglu(h, dense_w_gate[i], dense_w_up[i], dense_w_down[i])
        else:
            i = layer // 2
            f = moe_swiglu(h, router_w[i], router_b[i], moe_w_gate[i], moe_w_up[i], moe_w_down[i])
        x = x + f
    return rmsnorm(x, norm_final)


_drawn_inputs = setup_inputs


def setup_inputs(seed=0):
    import zlib

    import numpy as np

    out = dict(_drawn_inputs(seed))
    spreads = {}
    factors = {'ssm_a_re': 8.0, 'router_b': 3.848, 'norm_final': 2.802}
    for name, (base, spread) in spreads.items():
        noise = np.random.default_rng([zlib.crc32(name.encode()), seed]).standard_normal(out[name].shape)
        drawn = base * np.exp(spread * noise) if base else spread * noise
        out[name] = __import__('jax').numpy.asarray(drawn.astype(out[name].dtype))
    for name, factor in factors.items():
        out[name] = (out[name] * factor).astype(out[name].dtype)
    return out
```

```python
import concourse.bass as bass
from concourse import mybir
from contextlib import ExitStack


def hybrid_encoder_kernel(
    nc, x, norm_mix, w_in, b_in, conv_w, w_conv_out, ssm_a_re, ssm_a_im, ssm_log_dt,
    ssm_b_re, ssm_b_im, ssm_c_re, ssm_c_im, ssm_d, w_glu, w_o, norm_ffn,
    dense_w_gate, dense_w_up, dense_w_down, router_w, router_b,
    moe_w_gate, moe_w_up, moe_w_down, norm_final, out,
):
    F32, F32R, I32, U32 = mybir.dt.float32, mybir.dt.float32r, mybir.dt.int32, mybir.dt.uint32
    ALU, ACT, AX = mybir.AluOpType, mybir.ActivationFunctionType, mybir.AxisListType

    P = 128
    T = x.shape[1]
    D = x.shape[2]
    L = w_in.shape[0]
    KC = D // P
    TH = T // P
    F = dense_w_gate.shape[2]
    E = moe_w_gate.shape[1]
    NS = ssm_a_re.shape[2]
    G = ssm_a_re.shape[1]
    CG = ssm_b_re.shape[3]
    DS = G * CG
    NST = G * NS // P
    NU = DS // P
    H = T // 2
    HALF = 2048
    NB = F // 512
    RMS_EPS = 1e-6

    PV_B, PV_CONV, PV_NM, PV_NF, PV_D, PV_AR, PV_AI = 0, 44, 68, 76, 84, 88, 104
    PV_ROWS = 120
    PV_DT = PV_ROWS
    PV_N = PV_ROWS + NST

    KINDS = (["u"] * 2 + ["c", "v"] * 4 + ["b"] * 4 + ["gc"] * 4 + ["gs"] * 4
             + ["o"] * 4 + ["G"] * 2 + ["V"] * 2 + ["w"] * 4)
    NSTEP = len(KINDS)
    INDEX = [KINDS[:s].count(k) for s, k in enumerate(KINDS)]
    AT = {(k, i): s for s, (k, i) in enumerate(zip(KINDS, INDEX))}
    COL0 = {"b": 0, "c": D, "v": 2 * D, "u": 3 * D, "gc": 3 * D + DS, "gs": 4 * D + DS}
    BY_ACT = ("u", "c", "gc", "gs", "G")
    FFN_STEPS = 6 * NB
    BASE = [0, NSTEP + FFN_STEPS]
    MOE0 = 2 * NSTEP + FFN_STEPS
    ITEM = 6 * NB
    RAW, SPL = 6, 3
    BC_AT = [3, 2]
    BU_AT = [3 + 2 * q for q in range(8)]
    Y_AT = [7 + 2 * q for q in range(8)]
    GELU_AT = [14, 22]
    YSPLIT_AT = 24
    PAIR = [(q, q + 4) if q < 4 else (q + 4, q + 8) for q in range(8)]

    STAT_BANK = [7, 7, 3, 7]

    def bank_of(s):
        return (s % 2) * 2 + (s // 2) % 2

    ctx = ExitStack()
    with ctx:
        def sb(name, shape, dt=F32):
            return ctx.enter_context(nc.sbuf_tensor(name, shape, dt))

        def sem(name):
            return ctx.enter_context(nc.semaphore(name))

        raw = sb("raw", [P, RAW, HALF])
        whi = sb("whi", [P, SPL, HALF], F32R)
        wlo = sb("wlo", [P, SPL, HALF], F32R)
        FR = sb("fr", [P, 4 * 2048], F32R)
        used = [0]
        FP = sb("fp", [P, 18192 + 256])

        def take(n):
            used[0] += n
            return FP[:, used[0] - n:used[0]]

        def v3(ap, a):
            return ap.rearrange("p (a n) -> p a n", a=a)

        hH, hL = v3(FR[:, 0:2048], KC), v3(FR[:, 2048:4096], KC)
        pH, pL = v3(FR[:, 4096:6144], KC), v3(FR[:, 6144:8192], KC)
        yH, yL = v3(FR[:, 0:1024], NU), v3(FR[:, 2048:3072], NU)
        fH, fL = v3(FR[:, 4096:5120], 4), v3(FR[:, 6144:7168], 4)
        xgH, xgL = v3(FR[:, 0:1024], KC), v3(FR[:, 1024:2048], KC)
        tH, tL = v3(FR[:, 2048:2560], 4), v3(FR[:, 2560:3072], 4)
        zeroR = FR[:, 3072:3200]
        xT = v3(take(2048), KC)
        regC = take(2048)
        regU = take(KC * (T + 2))
        regTab = take(4096)
        regUT = take(1024)
        regZ = take(2048)
        regS = take(1024)
        tmpD = take(512)
        tmpP = take(512)
        ytmp = take(768)
        BTr, BTi, CTr, CTi = (v3(take(512), NU) for _ in range(4))
        cT = v3(regC, KC)
        hf = cT
        ucv = v3(regU, KC)
        gsT = ucv[:, :, 0:T]
        uT = v3(regUT, NU)
        cosT, sinT = v3(regTab[:, 0:2048], NST), v3(regTab[:, 2048:4096], NST)
        zr = v3(regZ[:, 0:1024], 2)
        zi = v3(regZ[:, 1024:2048], 2)
        sr, si = regS[:, 0:512], regS[:, 512:1024]
        braw = [v3(regS[:, 256 * i:256 * i + 256], NST) for i in range(2)]
        craw = [v3(regS[:, 512 + 256 * i:768 + 256 * i], NU) for i in range(2)]
        tgF, sgF, hbF = v3(regZ[:, 0:1024], 2), v3(regZ[:, 1024:2048], 2), v3(regUT, 2)
        htok = v3(regU[:, 0:2048], TH)
        acc = v3(regTab[:, 0:2048], TH)
        gfin = regTab[:, 2048:3072]
        tgM, sgM, hhM = regZ[:, 0:512], regZ[:, 512:1024], regZ[:, 1024:1536]
        PM, PT = v3(regZ[:, 1536:1792], TH), regZ[:, 1792:2048]
        ysc = regS
        fin = v3(regC, TH)
        xin = v3(regZ, TH)

        pv = sb("pv", [P, L, PV_N])
        pvh = sb("pvh", [P, L, 16])
        ident = sb("ident", [P, P])
        tri = sb("tri", [P, P])
        onesM = sb("ones", [P, P])
        iota = sb("iota", [P, P])
        par = sb("par", [P, 2])
        pid = sb("pid", [P, 1], I32)
        KL = L * NST
        mag = sb("mag", [P, KL])
        pwr = sb("pwr", [P, 8, KL])
        pwi = sb("pwi", [P, 8, KL])
        cfr = sb("cfr", [P, KL])
        cfi = sb("cfi", [P, KL])
        rw = sb("rw", [P, KC, E])
        nst = sb("nst", [P, 16])
        moe = sb("moe", [P, 64 + 16 * 8])
        rkI = v3(sb("rki", [P, 2 * 12])[:, :], 2)
        gI = v3(sb("gi", [P, 2 * 12])[:, :], 2)
        meta = sb("meta", [P, 4], I32)
        gcur = sb("gcur", [P, 2])
        gslot = sb("gslot", [P, 1])
        zb = sb("zb", [P, 12])

        ps = ctx.enter_context(nc.psum_tensor("ps", [P, 8, 512], F32))

        raw_full = [sem(f"raw_full{i}") for i in range(RAW)]
        hi_ready, lo_ready, unit_used = sem("hi_ready"), sem("lo_ready"), sem("unit_used")
        x_in, par_in, bc_in, out_done = sem("x_in"), sem("par_in"), sem("bc_in"), sem("out_done")
        late_in, zero_ready = sem("late_in"), sem("zero_ready")
        phase_ready = sem("phase_ready")
        consts = sem("consts")
        pool_chain, dve_chain, act_chain = sem("pool_chain"), sem("dve_chain"), sem("act_chain")
        ldt_ready = sem("ldt_ready")
        xt_ps, pv_ps, pv_ready, x_copied = sem("xt_ps"), sem("pv_ps"), sem("pv_ready"), sem("x_copied")
        coef_ready, bprep, cprep, bt_ps, ct_ps, bct_ready = (
            sem(n) for n in ("coef_ready", "bprep", "cprep", "bt_ps", "ct_ps", "bct_ready"))
        sq_ready, stat_ps, diag_ready, bc_ps, hf_ready, hh_ready, hl_ready = (
            sem(n) for n in ("sq_ready", "stat_ps", "diag_ready", "bc_ps", "hf_ready", "hh_ready", "hl_ready"))
        free_act, free_dve = sem("free_act"), sem("free_dve")
        gate_ready, ph_ready, pl_ready = sem("gate_ready"), sem("ph_ready"), sem("pl_ready")
        tab_ready, bu_ps, rot_done, z_ready, s_ready, y_ps, yd_done, gin_ready, gact_ready, gelu_done = (
            sem(n) for n in ("tab_ready", "bu_ps", "rot_done", "z_ready", "s_ready", "y_ps", "yd_done",
                             "gin_ready", "gact_ready", "gelu_done"))
        yh_ready, yl_ready, gg_done, m_ready, mh_ready, ml_ready = (
            sem(n) for n in ("yh_ready", "yl_ready", "gg_done", "m_ready", "mh_ready", "ml_ready"))
        f_tanh, f_silu, f_hid, f_hi, f_lo, f_out = (
            sem(n) for n in ("f_tanh", "f_silu", "f_hid", "f_hi", "f_lo", "f_out"))
        r_logit, r_diff, r_tanh, r_sel, r_rank, r_meta, ht_ps, ht_ready, xa_ps, acc_init = (
            sem(n) for n in ("r_logit", "r_diff", "r_tanh", "r_sel", "r_rank", "r_meta", "ht_ps",
                             "ht_ready", "xa_ps", "acc_init"))
        e_sel, e_pt_ps, e_pt, e_xg_ps, e_xgh, e_xgl = (
            sem(n) for n in ("e_sel", "e_pt_ps", "e_pt", "e_xg_ps", "e_xgh", "e_xgl"))
        e_tanh, e_silu, e_hid, e_t_ps, e_thi, e_tlo, e_y, e_comb, e_acc = (
            sem(n) for n in ("e_tanh", "e_silu", "e_hid", "e_t_ps", "e_thi", "e_tlo", "e_y", "e_comb", "e_acc"))
        fin_sq, fin_ready = sem("fin_sq"), sem("fin_ready")

        def psum_free(l, s):
            if KINDS[s] in BY_ACT:
                return free_act, l * sum(k in BY_ACT for k in KINDS) + sum(k in BY_ACT for k in KINDS[:s + 1])
            return free_dve, (l * sum(k not in BY_ACT for k in KINDS)
                              + sum(k not in BY_ACT for k in KINDS[:s + 1]))

        def wait_for(eng, pair):
            eng.wait_ge(pair[0], pair[1])

        def half_unit(n0, rounds):
            return n0 if rounds is None else rounds * RAW + n0

        def split_hi(act, n0, rounds=None):
            slot, n = n0 % RAW, half_unit(n0, rounds)
            fills = 16 * (n0 // RAW + 1)
            act.wait_ge(raw_full[slot], fills if rounds is None else rounds * 16 + fills)
            if n0 >= SPL:
                act.wait_ge(unit_used, n - (SPL - 1))
            act.activation(whi[:, slot % SPL, :], raw[:, slot, :], ACT.Copy).then_inc(hi_ready, 1)

        def split_lo(dve, n0, rounds=None):
            slot, n = n0 % RAW, half_unit(n0, rounds)
            dve.wait_ge(hi_ready, n + 1)
            dve.tensor_tensor(wlo[:, slot % SPL, :], raw[:, slot, :],
                              whi[:, slot % SPL, :].bitcast(F32), ALU.subtract).then_inc(lo_ready, 1)

        def load(sp, n0, rounds, src, pattern, k):
            slot, n = n0 % RAW, half_unit(n0, rounds)
            if n0 >= RAW:
                sp.wait_ge(lo_ready, n - (RAW - 1))
            sp.dma_start(raw[:, slot, :].rearrange("p (k n) -> p k n", k=k),
                         src.rearrange(pattern, p=P)).then_inc(raw_full[slot], 16)

        vst = v3(regU[:, 0:256], 2)

        def parameter_rows(eng, l):
            rows = [(PV_B, b_in[l], 44), (PV_NM, norm_mix[l], KC), (PV_NF, norm_ffn[l], KC), (PV_D, ssm_d[l], NU)]
            eng.dma_start(ytmp[0:NST, 2 * l:2 * l + 2], ssm_log_dt[l].rearrange("(r g) -> r g", g=2)).then_inc(par_in, 16)
            for r0, src in ((PV_AR, ssm_a_re), (PV_AI, ssm_a_im)):
                eng.dma_start(vst[r0:r0 + NST, l, :],
                              src[l].rearrange("(r g) n -> r (g n)", g=2)).then_inc(par_in, 16)
            for r0, src, k in rows:
                eng.dma_start(vst[r0:r0 + k, l, :], src.rearrange("(r p) -> r p", p=P)).then_inc(par_in, 16)
            eng.dma_start(vst[PV_CONV:PV_CONV + 24, l, :],
                          conv_w[l].rearrange("w (r p) -> (w r) p", p=P)).then_inc(par_in, 16)

        block = ctx.enter_context(nc.Block())

        @block.sync
        def _(sp):
            parameter_rows(sp, 1)

            def mixer_loads(l):
                for s, (kind, i) in enumerate(zip(KINDS, INDEX)):
                    n = BASE[l] + s
                    if kind in COL0:
                        c0 = COL0[kind] + 256 * i
                        src, k = w_in[l, :, c0:c0 + 256], 8
                    elif kind == "o":
                        src, k = w_conv_out[l, :, 256 * i:256 * i + 256], 8
                    elif kind == "w":
                        src, k = w_o[l, :, 256 * i:256 * i + 256], 8
                    else:
                        c0 = 512 * i + (D if kind == "G" else 0)
                        src, k = w_glu[l, :, c0:c0 + 512], 4
                    load(sp, n, None, src, "(k p) n -> p k n", k)

            def ffn_load(n, rounds, name, b, i):
                if name == "d":
                    src = dense_w_down[0, bass.ds(b * 512 + i * 256, 256), :]
                    load(sp, n, rounds, src, "(k p) n -> p k n", 2)
                else:
                    w = dense_w_gate if name == "g" else dense_w_up
                    load(sp, n, rounds, w[0, :, bass.ds(b * 512 + i * 256, 256)], "(k p) n -> p k n", 8)

            mixer_loads(0)
            n0 = BASE[0] + NSTEP
            for j, (name, i) in enumerate([("g", 0), ("g", 1), ("u", 0), ("u", 1)]):
                ffn_load(n0 + j, None, name, 0, i)
            with sp.Fori(0, NB - 1) as r:
                for j, (name, i) in enumerate(LOOP_STEPS):
                    ffn_load(n0 + 4 + j, r, name, r + (0 if name == "d" else 1), i)
            for i in range(2):
                ffn_load(n0 + ITEM - 2 + i, None, "d", NB - 1, i)

            mixer_loads(1)

            def item_loads(item, e):
                def ld(n, rounds, name, b, i):
                    if name == "d":
                        src = moe_w_down[0, bass.ds(e, 1), bass.ds(b * 512 + i * 256, 256), :]
                        k = 2
                    else:
                        w = moe_w_gate if name == "g" else moe_w_up
                        src = w[0, bass.ds(e, 1), 512 * i:512 * i + 512, bass.ds(b * 512, 512)]
                        k = 4
                    load(sp, n, rounds, src, "a (k p) n -> p (a k) n", k)
                for j, (name, i) in enumerate(HEAD_STEPS):
                    ld(MOE0 + j, item * NB, name, 0, i)
                with sp.Fori(0, NB - 1) as r:
                    for j, (name, i) in enumerate(LOOP_STEPS):
                        ld(MOE0 + 4 + j, item * NB + r, name, r + (0 if name == "d" else 1), i)
                for i in range(2):
                    ld(MOE0 + ITEM - 2 + i, item * NB, "d", NB - 1, i)

            with sp.Fori(0, E) as e:
                item_loads(e, e)
            sp.wait_ge(r_meta, 1)
            n_over = sp.value_load(meta[0:1, 0:1], min_val=0, max_val=3)
            with sp.If(n_over > 0):
                with sp.Fori(0, n_over) as r:
                    e = sp.value_load(meta[0:1, bass.ds(r + 1, 1)], min_val=0, max_val=E - 1)
                    item_loads(r + E, e)
            for j in range(2):
                slot = (MOE0 + j) % RAW
                sp.wait_ge(lo_ready, n_over * ITEM + (MOE0 + E * ITEM + j - (RAW - 1)))
                sp.dma_start(raw[:, slot, 0:16], w_o[0, 0:P, 0:16]).then_inc(raw_full[slot], 16)

            for h in range(TH):
                sp.wait_ge(fin_ready, h + 1)
                sp.dma_start(out[0, h * P:h * P + P, :], fin[:, h, :]).then_inc(out_done, 16)
            sp.wait_ge(out_done, 16 * TH)

        @block.gpsimd
        def _(pool):
            n_chain = [0]

            def link(ins):
                n_chain[0] += 1
                ins.then_inc(pool_chain, 1)
                pool.wait_ge(pool_chain, n_chain[0])

            def mark(ins):
                n_chain[0] += 1
                ins.then_inc(pool_chain, 1)

            pool.dma_start(xin, x[0].rearrange("(h p) d -> p h d", p=P)).then_inc(x_in, 16)
            link(pool.memset(ident[:, :], 0.0))
            pool.affine_select(out=ident[:, :], in_=ident[:, :], compare_op=ALU.not_equal, fill=1.0,
                               base=0, pattern=[[-1, P]], channel_multiplier=1).then_inc(consts, 1)
            pool.memset(onesM[:, :], 1.0).then_inc(consts, 1)
            link(pool.memset(tri[:, :], 1.0))
            pool.affine_select(out=tri[:, :], in_=tri[:, :], compare_op=ALU.is_gt, fill=0.0,
                               base=0, pattern=[[1, P]], channel_multiplier=-1).then_inc(consts, 1)
            pool.iota(iota[:, :], pattern=[[1, P]], base=0, channel_multiplier=0,
                      allow_small_or_imprecise_dtypes=True).then_inc(consts, 1)
            pool.iota(pid[:, :], pattern=[[0, 1]], base=0, channel_multiplier=1).then_inc(consts, 1)

            def power(l, k):
                pr, pi = (w[:, k - 1, l * NST:(l + 1) * NST] for w in (pwr, pwi))
                er, ei = (w[:, k, l * NST:(l + 1) * NST] for w in (pwr, pwi))
                a, b, c, f, g = (tmpP[:, NST * i:NST * (i + 1)] for i in range(5))
                mark(pool.tensor_tensor(a, pr, pr, ALU.mult))
                mark(pool.tensor_tensor(b, pi, pi, ALU.mult))
                link(pool.tensor_tensor(c, pr, pi, ALU.mult))
                mark(pool.tensor_tensor(er, a, b, ALU.subtract))
                link(pool.tensor_tensor(f, a, b, ALU.add))
                mark(pool.tensor_scalar(g, f, -2.0, 4.0, ALU.mult, ALU.add))
                link(pool.tensor_scalar(f, f, -1.0, 2.0, ALU.mult, ALU.add))
                mark(pool.tensor_tensor(ei, c, g, ALU.mult))
                link(pool.tensor_tensor(er, er, f, ALU.mult))

            def double(l, k, m0, m1):
                w = 1 << k
                m = min(m1 - m0, 256 // w)
                for t0 in range(m0, m1, m):
                    ts = slice(t0, t0 + m)
                    er = pwr[:, k, l * NST + t0:l * NST + t0 + m].unsqueeze(2).to_broadcast([P, m, w])
                    ei = pwi[:, k, l * NST + t0:l * NST + t0 + m].unsqueeze(2).to_broadcast([P, m, w])
                    ta, tb = (tmpP[:, 256 * i:256 * i + m * w].rearrange("p (a n) -> p a n", a=m) for i in range(2))
                    c0, s0 = cosT[:, ts, 0:w], sinT[:, ts, 0:w]
                    c1, s1 = cosT[:, ts, w:2 * w], sinT[:, ts, w:2 * w]
                    mark(pool.tensor_tensor(c1, c0, er, ALU.mult))
                    mark(pool.tensor_tensor(s1, c0, ei, ALU.mult))
                    mark(pool.tensor_tensor(ta, s0, ei, ALU.mult))
                    link(pool.tensor_tensor(tb, s0, er, ALU.mult))
                    mark(pool.tensor_tensor(c1, c1, ta, ALU.subtract))
                    link(pool.tensor_tensor(s1, s1, tb, ALU.add))

            for n in range(2):
                pool.wait_ge(hi_ready, n + 1)
                pool.tensor_tensor(wlo[:, n, :], raw[:, n, :], whi[:, n, :].bitcast(F32), ALU.subtract).then_inc(lo_ready, 1)

            pool.wait_ge(phase_ready, 1)
            for l in range(L):
                if l:
                    pool.wait_ge(rot_done, 8 * l)
                link(pool.memset(cosT[:, :, 0:1], 1.0))
                link(pool.memset(sinT[:, :, 0:1], 0.0))
                NH = NST // 2
                for k in range(7):
                    if k > 0:
                        power(l, k)
                    if k < 4:
                        double(l, k, 0, NST)
                    else:
                        double(l, k, 0, NH)
                power(l, 7)
                pool.nop().then_inc(tab_ready, 1)
                rest = [[(4, NH, NST)], [(5, NH, NST)], [(6, NH, NH + 4)], [(6, NH + 4, NST)]]
                double(l, *rest[0][0])
                if l:
                    for (piece,) in rest[1:]:
                        double(l, *piece)
                    pool.nop().then_inc(tab_ready, 1)
                for q in range(8):
                    m0, m1 = PAIR[q]
                    buf = q % 2
                    C = cosT[:, m0:m1 + 1:4, :].unsqueeze(2).to_broadcast([P, 2, 2, H])
                    S = sinT[:, m0:m1 + 1:4, :].unsqueeze(2).to_broadcast([P, 2, 2, H])

                    def q4(ap):
                        return ap.rearrange("p (a b n) -> p a b n", a=2, b=2)
                    pool.wait_ge(z_ready, 8 * l + q + 1)
                    if q == 0:
                        pool.wait_ge(bct_ready, l + 1)
                    else:
                        pool.wait_ge(y_ps, 8 * l + q)
                    pool.tensor_tensor(q4(sr), C, q4(zr[:, buf, :]), ALU.mult).then_inc(pool_chain, 1)
                    pool.tensor_tensor(q4(si), S, q4(zr[:, buf, :]), ALU.mult).then_inc(pool_chain, 1)
                    n_chain[0] += 2
                    link(pool.tensor_tensor(q4(tmpP), S, q4(zi[:, buf, :]), ALU.mult))
                    link(pool.tensor_tensor(q4(sr), q4(sr), q4(tmpP), ALU.subtract))
                    link(pool.tensor_tensor(q4(tmpP), C, q4(zi[:, buf, :]), ALU.mult))
                    pool.tensor_tensor(q4(si), q4(si), q4(tmpP), ALU.add).then_inc(s_ready, 1)
                    pool.wait_ge(s_ready, 8 * l + q + 1)
                    if l == 0 and q < 3:
                        double(l, *rest[q + 1][0])
                        if q == 2:
                            pool.nop().then_inc(tab_ready, 1)
                if l + 1 < L:
                    pool.wait_ge(y_ps, 8 * (l + 1))
                    for i, (w, c) in enumerate(((ssm_b_re, ssm_c_re), (ssm_b_im, ssm_c_im))):
                        pool.dma_start(braw[i], w[l + 1].rearrange("(m g) n c -> (g n) m c", g=2)).then_inc(late_in, 16)
                        pool.dma_start(craw[i], c[l + 1].rearrange("(j g) c n -> (g c) j n", j=NU)).then_inc(late_in, 16)
            pool.wait_ge(y_ps, 8 * L)
            pool.dma_start(gfin, norm_final.rearrange("(a n) -> a n", a=1).to_broadcast([P, D])).then_inc(late_in, 16)
            pool.wait_ge(yl_ready, L)
            pool.memset(zeroR.bitcast(F32), 0.0).then_inc(zero_ready, 1)

        @block.scalar
        def _(act):
            n_chain = [0]

            def link(ins):
                n_chain[0] += 1
                ins.then_inc(act_chain, 1)
                act.wait_ge(act_chain, n_chain[0])

            parameter_rows(act, 0)
            for i, (w, c) in enumerate(((ssm_b_re, ssm_c_re), (ssm_b_im, ssm_c_im))):
                act.dma_start(braw[i], w[0].rearrange("(m g) n c -> (g n) m c", g=2)).then_inc(bc_in, 16)
                act.dma_start(craw[i], c[0].rearrange("(j g) c n -> (g c) j n", j=NU)).then_inc(bc_in, 16)
            act.dma_start(rw[:, :, :], router_w[0].rearrange("(k p) e -> p k e", p=P)).then_inc(bc_in, 16)
            act.dma_start(moe[:, 0:E], router_b[0:1, :].to_broadcast([P, E])).then_inc(bc_in, 16)

            def norm_squares(v):
                for i in range(4):
                    if v == 0:
                        act.wait_ge(x_copied, i + 1)
                    elif v == 2:
                        act.wait_ge(f_out, i + 1)
                    else:
                        wait_for(act, psum_free(v // 2, AT["w", i]))
                    act.activation(cT[:, 2 * i:2 * i + 2, :], xT[:, 2 * i:2 * i + 2, :], ACT.Square).then_inc(sq_ready, 1)

            def norm_hi(v):
                for i in range(4):
                    act.wait_ge(hf_ready, 4 * v + i + 1)
                    act.activation(hH[:, 2 * i:2 * i + 2, :], hf[:, 2 * i:2 * i + 2, :], ACT.Copy).then_inc(hh_ready, 1)

            def mixer(l):
                base = BASE[l]
                g0 = l * 10

                def early(s):
                    kind, i = KINDS[s], INDEX[s]
                    if kind not in BY_ACT:
                        return
                    b = bank_of(s)
                    if kind == "G":
                        b0 = (s % 2) * 2
                        act.wait_ge(unit_used, base + s + 1)
                        zg = (zr if i == 0 else zi).rearrange("p a n -> p (a n)")
                        ins = act.activation(zg, ps[:, b0:b0 + 2, :].rearrange("p a n -> p (a n)"), ACT.Tanh, scale=0.5)
                        ins.then_inc(free_act, 1)
                        wait_for(act, psum_free(l, s))
                        act.activation(zg, zg, ACT.Copy, scale=0.5, bias=0.5).then_inc(gate_ready, 1)
                        return
                    act.wait_ge(unit_used, base + s + 1)
                    if kind == "gc":
                        wait_for(act, psum_free(l, AT["b", i]))
                    if kind == "gs":
                        act.wait_ge(pl_ready, 4 * l + i + 1)
                    for j in range(2):
                        t = 2 * i + j
                        src = ps[:, b, 256 * j:256 * j + 256]
                        col = COL0[kind] // P + t
                        if kind in ("u", "c"):
                            dst = uT[:, t, :] if kind == "u" else cT[:, t, :]
                            ins = act.activation(dst, src, ACT.Identity, bias=pv[:, l, PV_B + col:PV_B + col + 1])
                        else:
                            dst = cT[:, t, :] if kind == "gc" else gsT[:, t, :]
                            hcol = t + (0 if kind == "gc" else 8)
                            ins = act.activation(dst, src, ACT.Tanh, scale=0.5, bias=pvh[:, l, hcol:hcol + 1])
                    ins.then_inc(free_act, 1)
                    if kind in ("gc", "gs"):
                        wait_for(act, psum_free(l, s))
                        dst = (cT if kind == "gc" else gsT)[:, 2 * i:2 * i + 2, :]
                        act.activation(dst, dst, ACT.Copy, scale=0.5, bias=0.5).then_inc(gate_ready, 1)

                def late(s):
                    kind, i = KINDS[s], INDEX[s]
                    if kind == "b":
                        wait_for(act, psum_free(l, s))
                        act.activation(pH[:, 2 * i:2 * i + 2, :], gsT[:, 2 * i:2 * i + 2, :], ACT.Copy).then_inc(ph_ready, 1)
                    if kind == "V":
                        for j in range(2):
                            act.wait_ge(m_ready, 4 * l + 2 * i + j + 1)
                            t = 4 * i + 2 * j
                            act.activation(pH[:, t:t + 2, :], gsT[:, t:t + 2, :], ACT.Copy).then_inc(mh_ready, 1)

                for s in range(NSTEP + 1):
                    if s > 0:
                        early(s - 1)
                    if s < NSTEP:
                        split_hi(act, base + s + 2)
                    if s > 0:
                        late(s - 1)
                    if s in GELU_AT:
                        gi = GELU_AT.index(s)
                        act.wait_ge(gin_ready, 2 * l + gi + 1)
                        link(act.activation(ytmp[:, 0:512], ytmp[:, 0:512], ACT.Tanh, scale=0.7978845608028654))
                        act.activation(ytmp[:, 0:512], ytmp[:, 0:512], ACT.Copy, scale=0.5, bias=0.5).then_inc(gact_ready, 1)
                    if s == YSPLIT_AT:
                        act.wait_ge(gelu_done, 2 * (l + 1))
                        act.wait_ge(unit_used, base + AT["gs", 3] + 1)
                        act.activation(yH, uT, ACT.Copy).then_inc(yh_ready, 1)

            for i in range(4):
                act.wait_ge(xt_ps, i + 1)
                act.activation(xT[:, 2 * i:2 * i + 2, :].rearrange("p a n -> p (a n)"), ps[:, i, :], ACT.Copy).then_inc(x_copied, 1)
                if i < 2:
                    split_hi(act, i)
            norm_squares(0)
            norm_hi(0)
            mixer(0)
            norm_squares(1)
            norm_hi(1)

            n0 = NSTEP

            def f_tanh_step(blk, i, n):
                act.wait_ge(unit_used, n + 1)
                act.activation(tgF[:, i, :], ps[:, i, :], ACT.Tanh, scale=0.5).then_inc(f_tanh, 1)

            def f_hi_step(blk, i):
                act.wait_ge(f_hid, blk * 2 + (i + 1))
                act.activation(fH[:, 2 * i:2 * i + 2, :].rearrange("p a n -> p (a n)"), hbF[:, i, :], ACT.Copy).then_inc(f_hi, 1)

            def ffn_slot(blk, r, j):
                n = half_unit(n0 + 4 + j, r)
                if j in (1, 2):
                    f_tanh_step(blk, j - 1, n - 1)
                split_hi(act, n0 + 4 + j + 2, r)
                if j == 0:
                    f_hi_step(blk - 1, 1)
                if j == 5:
                    f_hi_step(blk, 0)

            for j, (name, i) in enumerate(HEAD_STEPS):
                if j in (1, 2):
                    f_tanh_step(0, j - 1, n0 + j - 1)
                split_hi(act, n0 + j + 2)
                if j == 3:
                    f_hi_step(0, 0)
            with act.Fori(0, NB - 1) as r:
                for j in range(6):
                    ffn_slot(r + 1, r, j)
            for j in range(2):
                split_hi(act, n0 + ITEM + j)
                if j == 0:
                    f_hi_step(NB - 1, 1)

            norm_squares(2)
            norm_hi(2)
            mixer(1)
            norm_squares(3)

            for b in range(4):
                act.wait_ge(ht_ps, b + 1)
                act.activation(htok[:, b // 2, 512 * (b % 2):512 * (b % 2) + 512], ps[:, b, :], ACT.Copy).then_inc(ht_ready, 1)
            act.wait_ge(r_diff, 1)
            act.activation(moe[:, 8:10], moe[:, 10:12], ACT.Tanh, scale=0.5).then_inc(r_tanh, 1)
            for b in range(4):
                act.wait_ge(xa_ps, b + 1)
                bank = (4, 5, 0, 1)[b]
                act.activation(acc[:, b // 2, 512 * (b % 2):512 * (b % 2) + 512], ps[:, bank, :], ACT.Copy).then_inc(acc_init, 1)
            act.wait_ge(e_xg_ps, 1)
            act.activation(FR[:, 0:1024], ps[:, 5:7, :].rearrange("p a n -> p (a n)"), ACT.Copy).then_inc(e_xgh, 1)
            act.wait_ge(r_meta, 1)
            n_over = act.value_load(meta[0:1, 0:1], min_val=0, max_val=3)
            with act.Fori(0, n_over + E) as item:
                m = item * ITEM + MOE0

                def tanh_step(q, n):
                    act.wait_ge(unit_used, n)
                    act.activation(tgM, ps[:, 0, :], ACT.Tanh, scale=0.5).then_inc(e_tanh, 1)

                def thi_step(q):
                    act.wait_ge(e_t_ps, q + 1)
                    act.activation(FR[:, 2048:2560], ps[:, 2, :], ACT.Copy).then_inc(e_thi, 1)

                for j in range(4):
                    if j == 1:
                        act.wait_ge(e_pt_ps, item + 1)
                        act.activation(PT, ps[:, 7, 0:256], ACT.Copy).then_inc(e_pt, 1)
                        act.activation(gslot[:, :], ps[:, 7, 256:257], ACT.Copy).then_inc(e_pt, 1)
                    if j == 2:
                        tanh_step(item * NB, m + 2)
                    split_hi(act, MOE0 + j + 2, item * NB)
                with act.Fori(0, NB - 1) as r:
                    mm = m + r * 6
                    for j in range(6):
                        if j == 1:
                            thi_step(item * NB + r)
                        if j == 2:
                            tanh_step(item * NB + (r + 1), mm + 6)
                        split_hi(act, MOE0 + j + 6, item * NB + r)
                thi_step(item * NB + (NB - 1))
                act.wait_ge(e_xg_ps, item + 2)
                act.activation(FR[:, 0:1024], ps[:, 5:7, :].rearrange("p a n -> p (a n)"), ACT.Copy).then_inc(e_xgh, 1)
                for j in range(2):
                    split_hi(act, MOE0 + ITEM + j, item * NB)
                act.wait_ge(unit_used, m + ITEM)
                act.wait_ge(e_pt, item * 2 + 2)
                act.activation(ysc, ps[:, 3:5, :].rearrange("p a n -> p (a n)"), ACT.Copy,
                               scale=gslot[:, 0:1]).then_inc(e_y, 1)

            act.wait_ge(e_acc, n_over * 4 + 4 * E)
            for h in range(TH):
                act.activation(fin[:, h, :], acc[:, h, :], ACT.Square, accum_out=nst[:, h:h + 1]).then_inc(fin_sq, 1)

        @block.vector
        def _(dve):
            n_chain = [0]

            def link(ins):
                n_chain[0] += 1
                ins.then_inc(dve_chain, 1)
                dve.wait_ge(dve_chain, n_chain[0])

            def mark(ins):
                n_chain[0] += 1
                ins.then_inc(dve_chain, 1)
                return n_chain[0]

            def tt(o, a, b, op):
                return dve.tensor_tensor(o, a, b, op)

            def stt(o, a, s, b, op0, op1):
                return dve.scalar_tensor_tensor(out=o, in0=a, scalar=s, in1=b, op0=op0, op1=op1)

            def ts(o, a, s1, op0, s2=None, op1=None):
                if op1 is None:
                    return dve.tensor_scalar(o, a, s1, None, op0)
                return dve.tensor_scalar(o, a, s1, s2, op0, op1)

            MUL, ADD, SUB = ALU.mult, ALU.add, ALU.subtract

            def inv_sqrt(y, v, a, b):
                link(ts(a.bitcast(I32), v.bitcast(I32), 1, ALU.logical_shift_right))
                link(ts(y.bitcast(I32), a.bitcast(I32), -1.0, MUL, float(0x5F3759DF), ADD))
                link(ts(b, v, -0.5, MUL))
                for _ in range(3):
                    link(tt(a, y, y, MUL))
                    link(tt(a, a, b, MUL))
                    link(stt(y, a, 1.5, y, ADD, MUL))

            dve.wait_ge(consts, 5)
            dve.wait_ge(par_in, 16 * 8 * L)
            ldx = ytmp[0:NST, 64:64 + L * P].rearrange("p (l g n) -> p (l g) n", l=L, g=2)
            dve.tensor_copy(ldx, ytmp[0:NST, 0:2 * L].unsqueeze(2).to_broadcast([NST, 2 * L, P // 2])).then_inc(ldt_ready, 1)

            dve.wait_ge(pv_ps, 1)
            link(dve.tensor_copy(pv[:, :, :], v3(ps[:, 6, 0:L * PV_N], L)))

            w2 = 2 * KL
            nxt = [1024]

            def t(n=KL):
                nxt[0] += n
                return regU[:, nxt[0] - n:nxt[0]]

            def lay(ap):
                return ap.rearrange("p (l m) -> p l m", l=L)
            ar, ai, dt2, x2, q2, r2, p2, n2, e2 = t(), t(), t(), t(), t(w2), t(w2), t(w2), t(w2), t()
            s1, s2, s3 = t(w2), t(w2), t(w2)
            sn, cs = p2[:, 0:KL], p2[:, KL:w2]

            def exp(o, a):
                    k, r, p, b = s1[:, 0:KL], s2[:, 0:KL], s3[:, 0:KL], s1[:, KL:w2]
                    link(ts(k, a, 1.4426950408889634, MUL))
                    link(ts(k, k, -126.0, ALU.max, 127.0, ALU.min))
                    link(dve.tensor_copy(b.bitcast(I32), k))
                    link(dve.tensor_copy(k, b.bitcast(I32)))
                    link(stt(r, k, -0.693359375, a, MUL, ADD))
                    link(stt(r, k, 2.12194440e-4, r, MUL, ADD))
                    link(ts(p, r, 1.0 / 40320, MUL))
                    for c in (5040, 720, 120, 24, 6, 2, 1):
                        link(stt(p, p, 1.0 / c, r, ADD, MUL))
                    link(ts(b.bitcast(I32), b.bitcast(I32), 127.0, ADD))
                    link(ts(b.bitcast(I32), b.bitcast(I32), 23, ALU.logical_shift_left))
                    link(stt(o, p, 1.0, b, ADD, MUL))

            def phases():
                mark(dve.tensor_copy(lay(ar), pv[:, :, PV_AR:PV_AR + NST]))
                mark(dve.tensor_copy(lay(ai), pv[:, :, PV_AI:PV_AI + NST]))
                link(dve.tensor_copy(lay(x2), pv[:, :, PV_DT:PV_DT + NST]))
                exp(dt2, x2)
                th = q2
                link(tt(th[:, 0:KL], ai, dt2, MUL))
                link(dve.tensor_copy(th[:, KL:w2], th[:, 0:KL]))
                link(ts(s1[:, 0:KL], th[:, 0:KL], 0.3183098861837907, MUL))
                link(ts(s1[:, KL:w2], th[:, KL:w2], 0.3183098861837907, MUL, -0.5, ADD))
                link(dve.tensor_copy(n2.bitcast(I32), s1))
                link(dve.tensor_copy(s1, n2.bitcast(I32)))
                link(ts(s1[:, KL:w2], s1[:, KL:w2], 0.5, ADD))
                link(stt(r2, s1, -3.140625, th, MUL, ADD))
                link(stt(r2, s1, -9.67502593994140625e-4, r2, MUL, ADD))
                link(stt(r2, s1, -1.509957990978376432e-7, r2, MUL, ADD))
                link(tt(s2, r2, r2, MUL))
                link(ts(p2, s2, 1.0 / 6227020800, MUL))
                for c in (-39916800, 362880, -5040, 120, -6):
                    link(stt(p2, p2, 1.0 / c, s2, ADD, MUL))
                link(stt(p2, p2, 1.0, r2, ADD, MUL))
                link(ts(n2.bitcast(I32), n2.bitcast(I32), 1, ALU.bitwise_and))
                link(dve.tensor_copy(s1, n2.bitcast(I32)))
                link(ts(s1[:, 0:KL], s1[:, 0:KL], -2.0, MUL, 1.0, ADD))
                link(ts(s1[:, KL:w2], s1[:, KL:w2], 2.0, MUL, -1.0, ADD))
                link(tt(p2, p2, s1, MUL))
                a, b = s1[:, 0:KL], s1[:, KL:w2]
                mark(tt(a, cs, cs, MUL))
                link(tt(b, sn, sn, MUL))
                link(tt(a, a, b, ADD))
                link(ts(a, a, -0.5, MUL, 1.5, ADD))
                mark(tt(pwr[:, 0, :], cs, a, MUL))
                tt(pwi[:, 0, :], sn, a, MUL).then_inc(phase_ready, 1)

            def coefficients():
                a, b = s1[:, 0:KL], s1[:, KL:w2]
                link(tt(x2, ar, dt2, MUL))
                exp(mag[:, :], x2)
                nr, ni, den = e2, r2[:, 0:KL], r2[:, KL:w2]
                link(tt(nr, mag[:, :], cs, MUL))
                link(ts(nr, nr, -1.0, ADD))
                link(tt(ni, mag[:, :], sn, MUL))
                link(tt(a, ar, ar, MUL))
                link(tt(b, ai, ai, MUL))
                link(tt(den, a, b, ADD))
                link(dve.reciprocal(den, den))
                link(tt(a, nr, ar, MUL))
                link(tt(b, ni, ai, MUL))
                link(tt(a, a, b, ADD))
                link(tt(cfr[:, :], a, den, MUL))
                link(tt(a, ni, ar, MUL))
                link(tt(b, nr, ai, MUL))
                link(tt(a, a, b, SUB))
                dve.tensor_tensor(cfi[:, :], a, den, MUL).then_inc(coef_ready, 1)
                dve.wait_ge(coef_ready, 1)

            def prepare_bc(l):
                bd = [v3(regZ[:, 512 * i:512 * i + 512], NST) for i in range(2)]
                cx = [v3(regZ[:, 1024 + 512 * i:1536 + 512 * i], NU) for i in range(2)]
                ls = slice(l * NST, (l + 1) * NST)
                if l == 0:
                    dve.wait_ge(bc_in, 16 * 6)
                else:
                    dve.wait_ge(late_in, 16 * 4)
                kr = cfr[:, ls].unsqueeze(2).to_broadcast([P, NST, CG])
                ki = cfi[:, ls].unsqueeze(2).to_broadcast([P, NST, CG])
                ta, tb = v3(tmpD[:, 0:256], NST), v3(tmpD[:, 256:512], NST)
                link(dve.memset(regZ[:, 0:1024], 0.0))
                for i in range(2):
                    link(tt(ta, kr, braw[i], MUL))
                    link(tt(tb, ki, braw[1 - i], MUL))
                    for g in range(2):
                        rows = slice(64 * g, 64 * g + 64)
                        link(tt(bd[i][rows, :, CG * g:CG * g + CG], ta[rows], tb[rows], SUB if i == 0 else ADD))
                dve.nop().then_inc(bprep, 1)
                for i in range(2):
                    for g in range(2):
                        o = cx[i][:, :, NS * g:NS * g + NS]
                        if i == 0:
                            link(ts(o, craw[i], par[:, g:g + 1], MUL))
                        else:
                            link(ts(o, craw[i], par[:, g:g + 1], MUL, -1.0, MUL))
                dve.nop().then_inc(cprep, 1)

            def finish_bc(l):
                dve.wait_ge(bt_ps, l + 1)
                link(dve.tensor_copy(BTr.rearrange("p a n -> p (a n)"), ps[:, 4, :]))
                link(dve.tensor_copy(BTi.rearrange("p a n -> p (a n)"), ps[:, 5, :]))
                dve.wait_ge(ct_ps, l + 1)
                link(dve.tensor_copy(CTr.rearrange("p a n -> p (a n)"), ps[:, 6, :]))
                dve.tensor_copy(CTi.rearrange("p a n -> p (a n)"), ps[:, 7, :]).then_inc(bct_ready, 1)
                dve.wait_ge(bct_ready, l + 1)

            def norm(v):
                if v == 2:
                    for i in range(4):
                        dve.wait_ge(unit_used, BASE[1])
                        dve.tensor_copy(xT[:, 2 * i:2 * i + 2, :].rearrange("p a n -> p (a n)"), ps[:, 4 + i, :]).then_inc(f_out, 1)
                dve.wait_ge(stat_ps, v + 1)
                link(ts(nst[:, 0:2], ps[:, STAT_BANK[v], 0:2], 1.0 / D, MUL, RMS_EPS, ADD))
                inv_sqrt(nst[:, 2:4], nst[:, 0:2], nst[:, 4:6], nst[:, 6:8])
                for h in range(TH):
                    ins = ts(tmpD[:, P * h:P * h + P], ident[:, :], nst[:, 2 + h:3 + h], MUL)
                    link(ins)
                dve.nop().then_inc(diag_ready, 1)
                dve.wait_ge(bc_ps, v + 1)
                pg = PV_NM if v % 2 == 0 else PV_NF

                def scaled(i):
                    for c in (2 * i, 2 * i + 1):
                        ins = stt(hf[:, c, :], xT[:, c, :], pv[:, v // 2, pg + c:pg + c + 1], ps[:, STAT_BANK[v], 256:512], MUL, MUL)
                    ins.then_inc(hf_ready, 1)

                def low(i):
                    dve.wait_ge(hh_ready, 4 * v + i + 1)
                    tt(hL[:, 2 * i:2 * i + 2, :], hf[:, 2 * i:2 * i + 2, :],
                       hH[:, 2 * i:2 * i + 2, :].bitcast(F32), SUB).then_inc(hl_ready, 1)
                scaled(0)
                for i in range(1, 4):
                    scaled(i)
                    if v < 3:
                        low(i - 1)
                if v < 3:
                    low(3)

            def rotate(l, q):
                m0, m1 = PAIR[q]
                buf = q % 2
                C = cosT[:, m0:m1 + 1:4, :].unsqueeze(2).to_broadcast([P, 2, 2, H])
                S = sinT[:, m0:m1 + 1:4, :].unsqueeze(2).to_broadcast([P, 2, 2, H])

                def q4(ap):
                    return ap.rearrange("p (a b n) -> p a b n", a=2, b=2)
                br, bi = q4(ps[:, 4, :]), q4(ps[:, 5, :])
                Zr, Zi, tm = q4(zr[:, buf, :]), q4(zi[:, buf, :]), q4(tmpD)
                dve.wait_ge(bu_ps, 8 * l + q + 1)
                if q % 4 == 0:
                    dve.wait_ge(tab_ready, 2 * l + q // 4 + 1)
                if q >= 2:
                    dve.wait_ge(s_ready, 8 * l + q - 1)
                a = mark(tt(Zr, C, br, MUL))
                b = mark(tt(Zi, C, bi, MUL))
                link(tt(tm, S, bi, MUL))
                link(tt(Zr, Zr, tm, ADD))
                link(tt(tm, S, br, MUL))
                ins = tt(Zi, Zi, tm, SUB)
                ins.then_inc(rot_done, 1)
                dve.wait_ge(rot_done, 8 * l + q + 1)
                mg = [mag[:, l * NST + m:l * NST + m + 1].to_broadcast([P, H]) for m in (m0, m1)]
                last = 0
                for a in range(2):
                    for z in (zr, zi):
                        o = z[:, buf, T * a:T * a + H]
                        last = mark(dve.tensor_tensor_scan(o, mg[a], o, 0.0, MUL, ADD))
                dve.wait_ge(dve_chain, last)
                e_r = pwr[:, 7, l * NST + m0:l * NST + m1 + 1:4]
                e_i = pwi[:, 7, l * NST + m0:l * NST + m1 + 1:4]
                z_r = zr[:, buf, H - 1:H - 1 + T + 1:T]
                z_i = zi[:, buf, H - 1:H - 1 + T + 1:T]
                mark(tt(zb[:, 0:2], e_r, z_r, MUL))
                mark(tt(zb[:, 2:4], e_i, z_i, MUL))
                mark(tt(zb[:, 4:6], e_i, z_r, MUL))
                link(tt(zb[:, 6:8], e_r, z_i, MUL))
                mark(tt(zb[:, 8:10], zb[:, 0:2], zb[:, 2:4], SUB))
                link(tt(zb[:, 10:12], zb[:, 4:6], zb[:, 6:8], ADD))
                for a in range(2):
                    for k, z in enumerate((zr, zi)):
                        o = z[:, buf, T * a + H:T * a + T]
                        ins = dve.tensor_tensor_scan(o, mg[a], o, zb[:, 8 + 2 * k + a:9 + 2 * k + a], MUL, ADD)
                ins.then_inc(z_ready, 1)

            def gelu_in(l, gi):
                dve.wait_ge(y_ps, 8 * l + 4 * (gi + 1))
                for a in range(2):
                    j = 2 * gi + a
                    ins = stt(uT[:, j, :], uT[:, j, :], pv[:, l, PV_D + j:PV_D + j + 1],
                              ps[:, 6, T * a:T * a + T], MUL, ADD)
                    link(ins)
                dve.nop().then_inc(yd_done, 1)
                y2 = uT[:, 2 * gi:2 * gi + 2, :].rearrange("p a n -> p (a n)")
                g = ytmp[:, 0:512]
                link(tt(g, y2, y2, MUL))
                link(ts(g, g, 0.044715, MUL, 1.0, ADD))
                tt(g, g, y2, MUL).then_inc(gin_ready, 1)

            def gelu_out(l, gi):
                y2 = uT[:, 2 * gi:2 * gi + 2, :].rearrange("p a n -> p (a n)")
                dve.wait_ge(gact_ready, 2 * l + gi + 1)
                tt(y2, y2, ytmp[:, 0:512], MUL).then_inc(gelu_done, 1)

            def mixer(l):
                base = BASE[l]

                def early(s):
                    kind, i = KINDS[s], INDEX[s]
                    b = bank_of(s)
                    if kind == "v":
                        dve.wait_ge(unit_used, base + s + 1)
                        wait_for(dve, psum_free(l, AT["c", i]))
                        for j in range(2):
                            t = 2 * i + j
                            col = COL0["v"] // P + t
                            ins = stt(ucv[:, t, 2:2 + T], ps[:, b, T * j:T * j + T],
                                      pv[:, l, PV_B + col:PV_B + col + 1], cT[:, t, :], ADD, MUL)
                            if j == 0:
                                link(ins)
                        ins.then_inc(free_dve, 1)
                        wait_for(dve, psum_free(l, s))
                        for w in range(3):
                            for j in range(2):
                                t = 2 * i + j
                                cw = pv[:, l, PV_CONV + 8 * w + t:PV_CONV + 8 * w + t + 1]
                                if w == 0:
                                    ins = ts(cT[:, t, :], ucv[:, t, 0:T], cw, MUL)
                                else:
                                    ins = stt(cT[:, t, :], ucv[:, t, w:w + T], cw, cT[:, t, :], MUL, ADD)
                                k = mark(ins)
                            dve.wait_ge(dve_chain, k)
                    elif kind == "b":
                        dve.wait_ge(unit_used, base + s + 1)
                        for j in range(2):
                            t = 2 * i + j
                            ins = stt(gsT[:, t, :], ps[:, b, T * j:T * j + T],
                                      pv[:, l, PV_B + t:PV_B + t + 1], cT[:, t, :], ADD, MUL)
                        ins.then_inc(free_dve, 1)
                    elif kind == "o":
                        dve.wait_ge(unit_used, base + s + 1)
                        dve.wait_ge(gate_ready, 10 * l + i + 1)
                        g = cT[:, 2 * i:2 * i + 2, :].rearrange("p a n -> p (a n)")
                        tt(g, g, ps[:, b, :], MUL).then_inc(free_dve, 1)
                    elif kind == "G":
                        dve.wait_ge(gate_ready, 10 * l + 8 + i + 1)
                        zg = v3((zr if i == 0 else zi).rearrange("p a n -> p (a n)"), 4)
                        tt(gsT[:, 4 * i:4 * i + 4, :], gsT[:, 4 * i:4 * i + 4, :], zg, MUL).then_inc(gg_done, 1)
                    elif kind == "V":
                        dve.wait_ge(unit_used, base + s + 1)
                        dve.wait_ge(gg_done, 2 * l + i + 1)
                        wait_for(dve, psum_free(l, AT["o", 3]))
                        b0 = (s % 2) * 2
                        for j in range(2):
                            t = 4 * i + 2 * j
                            ins = tt(gsT[:, t:t + 2, :], gsT[:, t:t + 2, :], v3(ps[:, b0 + j, :], 2), MUL)
                            if j == 0:
                                k = mark(ins)
                        ins.then_inc(free_dve, 1)
                        dve.wait_ge(dve_chain, k)
                        for j in range(2):
                            t = 4 * i + 2 * j
                            if j == 1:
                                wait_for(dve, psum_free(l, s))
                            tt(gsT[:, t:t + 2, :], gsT[:, t:t + 2, :], cT[:, t:t + 2, :], ADD).then_inc(m_ready, 1)
                    elif kind == "w":
                        dve.wait_ge(unit_used, base + s + 1)
                        xx = xT[:, 2 * i:2 * i + 2, :].rearrange("p a n -> p (a n)")
                        tt(xx, xx, ps[:, b, :], ADD).then_inc(free_dve, 1)

                def late(s):
                    kind, i = KINDS[s], INDEX[s]
                    if kind == "b":
                        dve.wait_ge(ph_ready, 4 * l + i + 1)
                        tt(pL[:, 2 * i:2 * i + 2, :], gsT[:, 2 * i:2 * i + 2, :],
                           pH[:, 2 * i:2 * i + 2, :].bitcast(F32), SUB).then_inc(pl_ready, 1)
                    if kind == "V":
                        for j in range(2):
                            dve.wait_ge(mh_ready, 4 * l + 2 * i + j + 1)
                            t = 4 * i + 2 * j
                            tt(pL[:, t:t + 2, :], gsT[:, t:t + 2, :], pH[:, t:t + 2, :].bitcast(F32), SUB).then_inc(ml_ready, 1)

                for s in range(NSTEP + 1):
                    if s > 0:
                        early(s - 1)
                    if s == BC_AT[l]:
                        finish_bc(l)
                    if s in GELU_AT:
                        gelu_in(l, GELU_AT.index(s))
                    if s < NSTEP:
                        split_lo(dve, base + s + 2)
                    if s == 0 and l == 0:
                        coefficients()
                    if s == BC_AT[l] - 2:
                        if l == 0:
                            prepare_bc(0)
                        link(dve.memset(ucv[:, :, 0:2], 0.0))
                    if s > 0:
                        late(s - 1)
                    if s in BU_AT:
                        rotate(l, BU_AT.index(s))
                    if s in GELU_AT:
                        gelu_out(l, GELU_AT.index(s))
                    if s == YSPLIT_AT:
                        dve.wait_ge(yh_ready, l + 1)
                        tt(yL, uT, yH.bitcast(F32), SUB).then_inc(yl_ready, 1)

            phases()
            norm(0)
            mark(ts(pvh[:, :, :], pv[:, :, PV_B + 28:PV_B + 44], 0.5, MUL))
            link(ts(pid[:, :], pid[:, :], 4, ALU.logical_shift_right, 1, ALU.bitwise_and))
            link(dve.tensor_copy(par[:, 1:2], pid[:, :]))
            link(ts(par[:, 0:1], par[:, 1:2], -1.0, MUL, 1.0, ADD))
            dve.wait_ge(lo_ready, 2)
            mixer(0)
            norm(1)

            n0 = NSTEP

            def f_silu_step(blk, i):
                dve.wait_ge(f_tanh, blk * 2 + (i + 1))
                stt(sgF[:, i, :], tgF[:, i, :], 1.0, ps[:, i, :], ADD, MUL).then_inc(f_silu, 1)

            def f_hid_step(blk, i, n):
                dve.wait_ge(unit_used, n + 1)
                dve.wait_ge(f_silu, blk * 2 + (i + 1))
                stt(hbF[:, i, :], sgF[:, i, :], 0.5, ps[:, 2 + i, :], MUL, MUL).then_inc(f_hid, 1)

            def f_lo_step(blk, i):
                dve.wait_ge(f_hi, blk * 2 + (i + 1))
                tt(fL[:, 2 * i:2 * i + 2, :].rearrange("p a n -> p (a n)"), hbF[:, i, :],
                   fH[:, 2 * i:2 * i + 2, :].rearrange("p a n -> p (a n)").bitcast(F32), SUB).then_inc(f_lo, 1)

            for j in range(4):
                if j in (1, 2):
                    f_silu_step(0, j - 1)
                if j == 3:
                    f_hid_step(0, 0, n0 + 2)
                split_lo(dve, n0 + j + 2)
                if j == 3:
                    f_lo_step(0, 0)
            with dve.Fori(0, NB - 1) as r:
                for j in range(6):
                    n = r * 6 + (n0 + 4 + j)
                    if j == 0:
                        f_hid_step(r, 1, n - 1)
                    if j in (1, 2):
                        f_silu_step(r + 1, j - 1)
                    if j == 5:
                        f_hid_step(r + 1, 0, n - 1)
                    split_lo(dve, n0 + 4 + j + 2, r)
                    if j == 0:
                        f_lo_step(r, 1)
                    if j == 5:
                        f_lo_step(r + 1, 0)
            for j in range(2):
                n = n0 + ITEM - 2 + j
                if j == 0:
                    f_hid_step(NB - 1, 1, n - 1)
                split_lo(dve, n + 2)
                if j == 0:
                    f_lo_step(NB - 1, 1)

            norm(2)
            prepare_bc(1)
            mixer(1)
            norm(3)

            lg = v3(moe[:, 16:32], 2)
            mx = v3(moe[:, 32:48], 2)
            ix = v3(moe[:, 48:64], 2)
            oh0, oh1 = v3(moe[:, 64:80], 2), v3(moe[:, 80:96], 2)
            sel, gt = v3(moe[:, 96:112], 2), v3(moe[:, 112:128], 2)
            rk = v3(moe[:, 128:144], 2)
            t16, t16b = v3(moe[:, 144:160], 2), v3(moe[:, 160:176], 2)
            over, cs = moe[:, 176:184], moe[:, 184:192]
            dve.wait_ge(r_logit, 1)
            for h in range(2):
                link(tt(lg[:, h, :], ps[:, 7, 8 * h:8 * h + 8], moe[:, 0:E], ADD))
                link(dve.max(mx[:, h, :], lg[:, h, :]))
                link(dve.max_index(ix[:, h, :].bitcast(U32), mx[:, h, :], lg[:, h, :]))
            tt(moe[:, 10:12], mx[:, :, 0], mx[:, :, 1], SUB).then_inc(r_diff, 1)
            link(dve.tensor_copy(t16, ix.bitcast(U32)))
            for h in range(2):
                link(ts(oh0[:, h, :], iota[:, 0:E], t16[:, h, 0:1], ALU.is_equal))
                link(ts(oh1[:, h, :], iota[:, 0:E], t16[:, h, 1:2], ALU.is_equal))
            tt(sel, oh0, oh1, ADD).then_inc(r_sel, 1)
            dve.wait_ge(r_tanh, 1)
            link(ts(moe[:, 12:14], moe[:, 8:10], 0.5, MUL, 0.5, ADD))
            link(ts(moe[:, 14:16], moe[:, 8:10], -0.5, MUL, 0.5, ADD))
            for h in range(2):
                link(ts(gt[:, h, :], oh0[:, h, :], moe[:, 12 + h:13 + h], MUL))
                link(stt(gt[:, h, :], oh1[:, h, :], moe[:, 14 + h:15 + h], gt[:, h, :], MUL, ADD))
            dve.wait_ge(r_rank, 1)
            dve.wait_ge(r_sel, 1)
            link(stt(rk, v3(ps[:, 7, 32:48], 2), 1.0, sel, ADD, MUL))
            link(ts(rk, rk, -1.0, ADD))
            link(dve.tensor_copy(rkI[:, :, 0:E], rk))
            link(dve.tensor_copy(gI[:, :, 0:E], gt))
            link(dve.memset(rkI[:, :, E:12], -1.0))
            link(dve.memset(gI[:, :, E:12], 0.0))
            link(ts(over, ps[:, 7, 64:72], float(P), ALU.is_gt))
            link(dve.tensor_tensor_scan(cs, onesM[:, 0:E], over, 0.0, MUL, ADD))
            link(dve.tensor_copy(meta[:, 0:1], cs[:, E - 1:E]))
            link(ts(rk, rk, -float(P - 1), ADD))
            for j in range(3):
                mj = moe[:, 144:152]
                link(ts(mj, cs, float(j + 1), ALU.is_equal))
                link(tt(mj, mj, over, MUL))
                link(tt(moe[:, 152:160], mj, iota[:, 0:E], MUL))
                link(dve.reduce_sum(moe[:, 160:161], moe[:, 152:160], axis=AX.X))
                link(dve.tensor_copy(meta[:, 1 + j:2 + j], moe[:, 160:161]))
                for h in range(2):
                    link(tt(moe[:, 152:160], mj, rk[:, h, :], MUL))
                    link(dve.reduce_sum(moe[:, 160:161], moe[:, 152:160], axis=AX.X))
                    link(ts(rkI[:, h, E + j:E + j + 1], moe[:, 160:161], -1.0, ADD))
                    link(tt(moe[:, 152:160], mj, gt[:, h, :], MUL))
                    link(dve.reduce_sum(gI[:, h, E + j:E + j + 1], moe[:, 152:160], axis=AX.X))
            dve.nop().then_inc(r_meta, 1)

            def select_tokens(item):
                for h in range(2):
                    dve.tensor_scalar(PM[:, h, :], iota[:, :], rkI[:, h, item], None, ALU.is_equal).then_inc(e_sel, 1)
                dve.tensor_copy(gcur[:, :].unsqueeze(2), gI[:, :, item]).then_inc(e_sel, 1)

            def xg_lo(count):
                dve.wait_ge(e_xgh, count)
                tt(FR[:, 1024:2048], ps[:, 5:7, :].rearrange("p a n -> p (a n)"), FR[:, 0:1024].bitcast(F32),
                   SUB).then_inc(e_xgl, 1)

            select_tokens(slice(0, 1))
            xg_lo(1)
            n_over = dve.value_load(meta[0:1, 0:1], min_val=0, max_val=3)
            with dve.Fori(0, n_over + E) as item:
                m = item * ITEM + MOE0

                def silu_step(q):
                    dve.wait_ge(e_tanh, q + 1)
                    stt(sgM, tgM, 1.0, ps[:, 0, :], ADD, MUL).then_inc(e_silu, 1)

                def hid_step(q, n):
                    dve.wait_ge(unit_used, n)
                    dve.wait_ge(e_silu, q + 1)
                    stt(hhM, sgM, 0.5, ps[:, 1, :], MUL, MUL).then_inc(e_hid, 1)

                def tlo_step(q):
                    dve.wait_ge(e_thi, q + 1)
                    tt(FR[:, 2560:3072], ps[:, 2, :], FR[:, 2048:2560].bitcast(F32), SUB).then_inc(e_tlo, 1)

                for j in range(4):
                    if j == 1:
                        dve.wait_ge(e_pt_ps, item + 1)
                        select_tokens(bass.ds(item + 1, 1))
                    if j == 2:
                        silu_step(item * NB)
                    split_lo(dve, MOE0 + j + 2, item * NB)
                with dve.Fori(0, NB - 1) as r:
                    mm = m + r * 6
                    for j in range(6):
                        if j == 0:
                            hid_step(item * NB + r, mm + 4)
                        if j == 1:
                            tlo_step(item * NB + r)
                        if j == 2:
                            silu_step(item * NB + (r + 1))
                        split_lo(dve, MOE0 + j + 6, item * NB + r)
                hid_step(item * NB + (NB - 1), m + (ITEM - 2))
                tlo_step(item * NB + (NB - 1))
                xg_lo(item + 2)
                for j in range(2):
                    split_lo(dve, MOE0 + ITEM + j, item * NB)
                dve.wait_ge(acc_init, 4)
                for k, bank in enumerate(COMB_BANKS):
                    dve.wait_ge(e_comb, item * 4 + (k + 1))
                    dve.wait_ge(e_acc, item * 4)
                    a = acc[:, k // 2, 512 * (k % 2):512 * (k % 2) + 512]
                    tt(a, a, ps[:, bank, :], ADD).then_inc(e_acc, 1)

            dve.wait_ge(fin_sq, TH)
            link(ts(nst[:, 8:10], nst[:, 0:2], 1.0 / D, MUL, RMS_EPS, ADD))
            inv_sqrt(nst[:, 2:4], nst[:, 8:10], nst[:, 4:6], nst[:, 6:8])
            dve.wait_ge(late_in, 16 * 5)
            for h in range(TH):
                stt(fin[:, h, :], acc[:, h, :], nst[:, 2 + h:3 + h], gfin, MUL, MUL).then_inc(fin_ready, 1)

        @block.tensor
        def _(pe):
            pe.wait_ge(consts, 5)
            pe.wait_ge(ldt_ready, 1)
            for l in range(L):
                pe.transpose(ps[:, 6, l * PV_N:l * PV_N + PV_ROWS], vst[0:PV_ROWS, l, :], ident[0:PV_ROWS, 0:PV_ROWS])
                ins = pe.transpose(ps[:, 6, l * PV_N + PV_DT:l * PV_N + PV_N], ytmp[0:NST, 64 + l * P:64 + l * P + P],
                                   ident[0:NST, 0:NST])
            ins.then_inc(pv_ps, 1)
            pe.wait_ge(x_in, 16)
            for i in range(4):
                for c in (2 * i, 2 * i + 1):
                    for h in range(TH):
                        o = (c % 2) * T + h * P
                        ins = pe.transpose(ps[:, i, o:o + P], xin[:, h, c * P:c * P + P], ident[:, :])
                ins.then_inc(xt_ps, 1)

            def three(o, w_h, w_l, x_h, x_l, first, last):
                pe.matmul(o, w_h, x_h, start=first, stop=False, skip_group_check=True)
                pe.matmul(o, w_h, x_l, start=False, stop=False, skip_group_check=True)
                return pe.matmul(o, w_l, x_h, start=False, stop=last, skip_group_check=True)

            def norm(v):
                for i in range(4):
                    pe.wait_ge(sq_ready, 4 * v + i + 1)
                    for c in (2 * i, 2 * i + 1):
                        for h in range(TH):
                            ins = pe.matmul(ps[:, STAT_BANK[v], h:h + 1], cT[:, c, h * P:h * P + P], onesM[:, 0:1],
                                            start=(c == 0 and h == 0), stop=(c == KC - 1), skip_group_check=True)
                ins.then_inc(stat_ps, 1)
                pe.wait_ge(diag_ready, v + 1)
                for h in range(TH):
                    ins = pe.matmul(ps[:, STAT_BANK[v], T + h * P:T + h * P + P], onesM[:, :], tmpD[:, h * P:h * P + P],
                                    start=True, stop=True)
                ins.then_inc(bc_ps, 1)

            def prepare_bc(l):
                bd = [regZ[:, 512 * i:512 * i + 512] for i in range(2)]
                cx = [regZ[:, 1024 + 512 * i:1536 + 512 * i] for i in range(2)]
                pe.wait_ge(bprep, l + 1)
                for i in range(2):
                    for j in range(NU):
                        ins = pe.transpose(ps[:, 4 + i, P * j:P * j + P], bd[i][:, P * j:P * j + P], ident[:, :])
                ins.then_inc(bt_ps, 1)
                pe.wait_ge(cprep, l + 1)
                pe.wait_ge(hf_ready, 8 * l + 4)
                for i in range(2):
                    for j in range(NU):
                        ins = pe.transpose(ps[:, 6 + i, P * j:P * j + P], cx[i][:, P * j:P * j + P], ident[:, :])
                ins.then_inc(ct_ps, 1)

            def drive_states(l, q):
                wait_for(pe, psum_free(l, AT["u", 1]))
                pe.wait_ge(bct_ready, l + 1)
                if q > 0:
                    pe.wait_ge(rot_done, 8 * l + q)
                r = 32 * (q % 4)
                for a, m in enumerate(PAIR[q]):
                    for k, w in enumerate((BTr, BTi)):
                        ins = pe.matmul(ps[:, 4 + k, T * a:T * a + T], w[r:r + 32, m // 4, :], uT[r:r + 32, m // 4, :],
                                        start=True, stop=True)
                ins.then_inc(bu_ps, 1)

            def read_states(l, q):
                pe.wait_ge(s_ready, 8 * l + q + 1)
                if q == 4:
                    pe.wait_ge(yd_done, 2 * l + 1)
                r = 32 * (q % 4)
                for a, m in enumerate(PAIR[q]):
                    for k, (w, s) in enumerate(((CTr, sr), (CTi, si))):
                        ins = pe.matmul(ps[r:r + 32, 6, T * a:T * a + T], w[:, m // 4, r:r + 32], s[:, T * a:T * a + T],
                                        start=(k == 0), stop=(k == 1))
                ins.then_inc(y_ps, 1)

            def mixer(l):
                base = BASE[l]
                for s, (kind, i) in enumerate(zip(KINDS, INDEX)):
                    n = base + s
                    if s == BC_AT[l] - 1:
                        prepare_bc(l)
                    if s in BU_AT:
                        drive_states(l, BU_AT.index(s))
                    if s in Y_AT:
                        read_states(l, Y_AT.index(s))
                    pe.wait_ge(lo_ready, n + 1)
                    if s >= 2:
                        wait_for(pe, psum_free(l, s - 2))
                    slot = n % SPL
                    if kind in ("G", "V"):
                        pe.wait_ge(yl_ready, l + 1)
                        wh, wl = v3(whi[:, slot, :], 4), v3(wlo[:, slot, :], 4)
                        tiles = [(ps[:, (s % 2) * 2 + j // 2, T * (j % 2):T * (j % 2) + T], j) for j in range(4)]
                        kc, xh, xl = 4, yH, yL
                    else:
                        wh, wl = v3(whi[:, slot, :], 8), v3(wlo[:, slot, :], 8)
                        tiles = [(ps[:, bank_of(s), T * j:T * j + T], j) for j in range(2)]
                        kc, (xh, xl) = 8, ((hH, hL) if kind in COL0 else (pH, pL))
                    if kind == "o":
                        pe.wait_ge(pl_ready, 4 * (l + 1))
                    if kind == "w":
                        pe.wait_ge(ml_ready, 4 * (l + 1))
                    for o, j in tiles:
                        for k in range(kc):
                            if s == 0 and j == 0 and k % 2 == 0:
                                pe.wait_ge(hl_ready, 8 * l + k // 2 + 1)
                            cols = slice(P * j, P * j + P)
                            ins = three(o, wh[:, k, cols], wl[:, k, cols], xh[:, k, :], xl[:, k, :], k == 0, k == kc - 1)
                    ins.then_inc(unit_used, 1)

            norm(0)
            mixer(0)
            norm(1)

            n0 = NSTEP

            def up_or_gate(n, slot, bank, first_use=False):
                wh, wl = v3(whi[:, slot % SPL, :], 8), v3(wlo[:, slot % SPL, :], 8)
                pe.wait_ge(lo_ready, n + 1)
                for j in range(2):
                    for k in range(8):
                        if first_use and j == 0 and k % 2 == 0:
                            pe.wait_ge(hl_ready, 4 + k // 2 + 1)
                        cols = slice(P * j, P * j + P)
                        ins = three(ps[:, bank, T * j:T * j + T], wh[:, k, cols], wl[:, k, cols],
                                    hH[:, k, :], hL[:, k, :], k == 0, k == 7)
                ins.then_inc(unit_used, 1)

            def down(n, slot, blk, i, last=False):
                wh, wl = v3(whi[:, slot % SPL, :], 2), v3(wlo[:, slot % SPL, :], 2)
                pe.wait_ge(lo_ready, n + 1)
                pe.wait_ge(f_lo, blk * 2 + (i + 1))
                for j in range(KC):
                    for k in range(2):
                        cols = slice(P * j, P * j + P)
                        ins = three(ps[:, 4 + j // 2, T * (j % 2):T * (j % 2) + T], wh[:, k, cols], wl[:, k, cols],
                                    fH[:, 2 * i + k, :], fL[:, 2 * i + k, :], False, last and k == 1)
                ins.then_inc(unit_used, 1)

            for j, (name, i) in enumerate(HEAD_STEPS):
                n = n0 + j
                up_or_gate(n, n % RAW, j, first_use=(j == 0))
            pe.wait_ge(hf_ready, 8)
            for i in range(4):
                pe.matmul(ps[:, 4 + i, :], ident[:, :], xT[:, 2 * i:2 * i + 2, :], start=True, stop=False, skip_group_check=True)
            with pe.Fori(0, NB - 1) as r:
                for j, (name, i) in enumerate(LOOP_STEPS):
                    n = r * 6 + (n0 + 4 + j)
                    slot = (n0 + 4 + j) % RAW
                    if name == "g":
                        pe.wait_ge(f_silu, r * 2 + (i + 1))
                        up_or_gate(n, slot, i)
                    elif name == "u":
                        pe.wait_ge(f_hid, r * 2 + (i + 1))
                        up_or_gate(n, slot, 2 + i)
                    else:
                        down(n, slot, r, i)
            for i in range(2):
                down(n0 + ITEM - 2 + i, (n0 + ITEM - 2 + i) % RAW, NB - 1, i, last=(i == 1))

            norm(2)
            pe.wait_ge(f_out, 4)
            mixer(1)
            norm(3)

            pe.wait_ge(hf_ready, 16)
            pe.wait_ge(bc_in, 16 * 6)
            for h in range(TH):
                for c in range(KC):
                    ins = pe.matmul(ps[:, 7, E * h:E * h + E], hf[:, c, h * P:h * P + P], rw[:, c, :],
                                    start=(c == 0), stop=(c == KC - 1))
            ins.then_inc(r_logit, 1)
            wait_for(pe, psum_free(1, NSTEP - 1))
            for h in range(TH):
                for c in range(KC):
                    ins = pe.transpose(ps[:, 2 * h + c // 4, P * (c % 4):P * (c % 4) + P], hf[:, c, h * P:h * P + P], ident[:, :])
                    if c % 4 == 3:
                        ins.then_inc(ht_ps, 1)
            pe.wait_ge(r_sel, 1)
            sel = v3(moe[:, 96:112], 2)
            pe.matmul(ps[:, 7, 32:40], tri[:, :], sel[:, 0, :], start=True, stop=True)
            pe.matmul(ps[:, 7, 40:48], onesM[:, :], sel[:, 0, :], start=True, stop=False)
            pe.matmul(ps[:, 7, 40:48], tri[:, :], sel[:, 1, :], start=False, stop=True)
            pe.matmul(ps[:, 7, 64:72], onesM[:, :], sel[:, 0, :], start=True, stop=False)
            pe.matmul(ps[:, 7, 64:72], onesM[:, :], sel[:, 1, :], start=False, stop=True).then_inc(r_rank, 1)
            for b in range(4):
                h = b // 2
                bank = (4, 5, 0, 1)[b]
                if b == 2:
                    pe.wait_ge(ht_ready, 2)
                for c in range(4 * (b % 2), 4 * (b % 2) + 4):
                    ins = pe.transpose(ps[:, bank, P * (c % 4):P * (c % 4) + P], xT[:, c, h * P:h * P + P], ident[:, :])
                ins.then_inc(xa_ps, 1)

            def gather(count):
                pe.wait_ge(e_sel, count * 3)
                for c in range(KC):
                    for h in range(TH):
                        ins = pe.matmul(ps[:, 5 + c // 4, P * (c % 4):P * (c % 4) + P], htok[:, h, c * P:c * P + P],
                                        PM[:, h, :], start=(h == 0), stop=(h == TH - 1))
                ins.then_inc(e_xg_ps, 1)

            pe.wait_ge(ht_ready, 4)
            pe.wait_ge(acc_init, 4)
            gather(1)
            pe.wait_ge(r_meta, 1)
            n_over = pe.value_load(meta[0:1, 0:1], min_val=0, max_val=3)

            def expert_product(n, slot, bank, i):
                wh, wl = v3(whi[:, slot % SPL, :], 4), v3(wlo[:, slot % SPL, :], 4)
                pe.wait_ge(lo_ready, n + 1)
                for k in range(4):
                    o, c = ps[:, bank, :], 4 * i + k
                    pe.matmul(o, xgH[:, c, :], wh[:, k, :], start=(c == 0), stop=False, skip_group_check=True)
                    pe.matmul(o, xgH[:, c, :], wl[:, k, :], start=False, stop=False, skip_group_check=True)
                    ins = pe.matmul(o, xgL[:, c, :], wh[:, k, :], start=False, stop=(c == KC - 1), skip_group_check=True)
                ins.then_inc(unit_used, 1)

            def expert_down(n, slot, q, i, last=False):
                wh, wl = v3(whi[:, slot % SPL, :], 2), v3(wlo[:, slot % SPL, :], 2)
                pe.wait_ge(lo_ready, n + 1)
                pe.wait_ge(e_tlo, q + 1)
                for k in range(2):
                    for j in range(2):
                        o, c, cols = ps[:, 3 + j, :], 2 * i + k, slice(512 * j, 512 * j + 512)
                        pe.matmul(o, tH[:, c, :], wh[:, k, cols], start=False, stop=False, skip_group_check=True)
                        pe.matmul(o, tH[:, c, :], wl[:, k, cols], start=False, stop=False, skip_group_check=True)
                        ins = pe.matmul(o, tL[:, c, :], wh[:, k, cols], start=False, stop=last and c == 3, skip_group_check=True)
                ins.then_inc(unit_used, 1)

            def turn_hidden(q):
                pe.wait_ge(e_hid, q + 1)
                for c in range(4):
                    ins = pe.transpose(ps[:, 2, P * c:P * c + P], hhM[:, P * c:P * c + P], ident[:, :])
                ins.then_inc(e_t_ps, 1)

            with pe.Fori(0, n_over + E) as item:
                m = item * ITEM + MOE0
                q0 = item * NB
                pe.wait_ge(e_xgl, item + 1)
                for j, (name, i) in enumerate(HEAD_STEPS):
                    if j == 0:
                        pe.wait_ge(e_silu, q0)
                    if j == 2:
                        pe.wait_ge(e_hid, q0)
                    expert_product(m + j, (MOE0 + j) % RAW, 0 if name == "g" else 1, i)
                    if j == 0:
                        pe.wait_ge(e_acc, item * 4)
                        for h in range(TH):
                            pe.transpose(ps[:, 7, P * h:P * h + P], PM[:, h, :], ident[:, :])
                        pe.matmul(ps[:, 7, 256:257], PM[:, 0, :], gcur[:, 0:1], start=True, stop=False)
                        pe.matmul(ps[:, 7, 256:257], PM[:, 1, :], gcur[:, 1:2], start=False, stop=True).then_inc(e_pt_ps, 1)
                pe.wait_ge(zero_ready, 1)
                pe.wait_ge(e_y, item)
                for j in range(2):
                    pe.matmul(ps[:, 3 + j, :], zeroR, xgH[:, 0:4, :], start=True, stop=False, skip_group_check=True)
                with pe.Fori(0, NB - 1) as r:
                    mm = m + r * 6
                    q = q0 + r
                    for j, (name, i) in enumerate(LOOP_STEPS):
                        n, slot = mm + (4 + j), (MOE0 + 4 + j) % RAW
                        if j == 0:
                            pe.wait_ge(e_silu, q + 1)
                        if j == 4:
                            pe.wait_ge(e_hid, q + 1)
                        if name == "d":
                            expert_down(n, slot, q, i)
                        else:
                            expert_product(n, slot, 0 if name == "g" else 1, i)
                        if j == 0:
                            turn_hidden(q)
                gather(item + 2)
                turn_hidden(q0 + (NB - 1))
                for i in range(2):
                    expert_down(m + (ITEM - 2 + i), (MOE0 + ITEM - 2 + i) % RAW, q0 + (NB - 1), i, last=(i == 1))
                pe.wait_ge(e_y, item + 1)
                pe.wait_ge(e_pt, item * 2 + 2)
                pe.wait_ge(e_xgl, item + 2)
                for k, bank in enumerate(COMB_BANKS):
                    pe.matmul(ps[:, bank, :], PT[:, P * (k // 2):P * (k // 2) + P], ysc[:, 512 * (k % 2):512 * (k % 2) + 512],
                              start=True, stop=True).then_inc(e_comb, 1)


HEAD_STEPS = [("g", 0), ("g", 1), ("u", 0), ("u", 1)]
LOOP_STEPS = [("g", 0), ("g", 1), ("d", 0), ("d", 1), ("u", 0), ("u", 1)]
COMB_BANKS = (5, 6, 7, 2)


_INS = ["x", "norm_mix", "w_in", "b_in", "conv_w", "w_conv_out", "ssm_a_re", "ssm_a_im", "ssm_log_dt",
        "ssm_b_re", "ssm_b_im", "ssm_c_re", "ssm_c_im", "ssm_d", "w_glu", "w_o", "norm_ffn",
        "dense_w_gate", "dense_w_up", "dense_w_down", "router_w", "router_b",
        "moe_w_gate", "moe_w_up", "moe_w_down", "norm_final"]


def kernel(**inputs):
    import numpy as _np
    import concourse.bacc as _bacc
    from concourse import mybir as _mybir
    from concourse.bass_utils import run_bass_kernel_spmd as _run

    nc = _bacc.Bacc("TRN2", target_bir_lowering=False, num_devices=1)
    arrays, args = {}, []
    for name in _INS:
        a = _np.ascontiguousarray(inputs[name])
        arrays[f"in_{name}"] = a
        args.append(nc.dram_tensor(f"in_{name}", a.shape, _mybir.dt.from_np(a.dtype), kind="ExternalInput").ap())
    shape = inputs["x"].shape
    args.append(nc.dram_tensor("out_0", shape, _mybir.dt.float32, kind="ExternalOutput").ap())
    hybrid_encoder_kernel(nc, *args)
    r = _run(nc, [arrays], core_ids=[0])
    return r.results[0]["out_0"]
```

```python
import concourse.bass as bass
from concourse import mybir
from contextlib import ExitStack


def hybrid_encoder_kernel(
    nc, x, norm_mix, w_in, b_in, conv_w, w_conv_out, ssm_a_re, ssm_a_im, ssm_log_dt,
    ssm_b_re, ssm_b_im, ssm_c_re, ssm_c_im, ssm_d, w_glu, w_o, norm_ffn,
    dense_w_gate, dense_w_up, dense_w_down, router_w, router_b,
    moe_w_gate, moe_w_up, moe_w_down, norm_final, out,
):
    F32, F32R, I32, U32 = mybir.dt.float32, mybir.dt.float32r, mybir.dt.int32, mybir.dt.uint32
    ALU, ACT, AX = mybir.AluOpType, mybir.ActivationFunctionType, mybir.AxisListType

    P = 128
    T = x.shape[1]
    D = x.shape[2]
    L = w_in.shape[0]
    KC = D // P
    TH = T // P
    F = dense_w_gate.shape[2]
    E = moe_w_gate.shape[1]
    NS = ssm_a_re.shape[2]
    G = ssm_a_re.shape[1]
    CG = ssm_b_re.shape[3]
    DS = G * CG
    NST = G * NS // P
    NU = DS // P
    H = T // 2
    HALF = 2048
    NB = F // 512
    RMS_EPS = 1e-6

    PV_B, PV_CONV, PV_NM, PV_NF, PV_D, PV_AR, PV_AI = 0, 44, 68, 76, 84, 88, 104
    PV_ROWS = 120
    PV_DT = PV_ROWS
    PV_N = PV_ROWS + NST

    KINDS = (["u"] * 2 + ["c", "v"] * 4 + ["b"] * 4 + ["gc"] * 4 + ["gs"] * 4
             + ["o"] * 4 + ["G"] * 2 + ["V"] * 2 + ["w"] * 4)
    NSTEP = len(KINDS)
    INDEX = [KINDS[:s].count(k) for s, k in enumerate(KINDS)]
    AT = {(k, i): s for s, (k, i) in enumerate(zip(KINDS, INDEX))}
    COL0 = {"b": 0, "c": D, "v": 2 * D, "u": 3 * D, "gc": 3 * D + DS, "gs": 4 * D + DS}
    BY_ACT = ("u", "c", "gc", "gs", "G")
    FFN_STEPS = 6 * NB
    BASE = [0, NSTEP + FFN_STEPS]
    MOE0 = 2 * NSTEP + FFN_STEPS
    ITEM = 6 * NB
    RAW, SPL = 6, 3
    BC_AT = [3, 2]
    BU_AT = [3 + 2 * q for q in range(8)]
    Y_AT = [7 + 2 * q for q in range(8)]
    GELU_AT = [14, 22]
    YSPLIT_AT = 24
    PAIR = [(q, q + 4) if q < 4 else (q + 4, q + 8) for q in range(8)]

    XA_BANK = [4, 3, 2, 1]
    STAT_BANK = [7, 7, 3, 7]
    SUMMED = [4, 6, 4, 6]

    def bank_of(s):
        return (s % 2) * 2 + (s // 2) % 2

    ctx = ExitStack()
    with ctx:
        def sb(name, shape, dt=F32):
            return ctx.enter_context(nc.sbuf_tensor(name, shape, dt))

        def sem(name):
            return ctx.enter_context(nc.semaphore(name))

        raw = sb("raw", [P, RAW, HALF])
        whi = sb("whi", [P, SPL, HALF], F32R)
        wlo = sb("wlo", [P, SPL, HALF], F32R)
        FR = sb("fr", [P, 4 * 2048], F32R)
        used = [0]
        FP = sb("fp", [P, 18192 + 256])

        def take(n):
            used[0] += n
            return FP[:, used[0] - n:used[0]]

        def v3(ap, a):
            return ap.rearrange("p (a n) -> p a n", a=a)

        hH, hL = v3(FR[:, 0:2048], KC), v3(FR[:, 2048:4096], KC)
        pH, pL = v3(FR[:, 4096:6144], KC), v3(FR[:, 6144:8192], KC)
        yH, yL = v3(FR[:, 0:1024], NU), v3(FR[:, 2048:3072], NU)
        fH, fL = v3(FR[:, 4096:5120], 4), v3(FR[:, 6144:7168], 4)
        xgH, xgL = v3(FR[:, 0:1024], KC), v3(FR[:, 1024:2048], KC)
        tH, tL = v3(FR[:, 2048:2560], 4), v3(FR[:, 2560:3072], 4)
        zeroR = FR[:, 3072:3200]
        xT = v3(take(2048), KC)
        regC = take(2048)
        regU = take(KC * (T + 2))
        regTab = take(4096)
        regUT = take(1024)
        regZ = take(2048)
        regS = take(1024)
        tmpD = take(512)
        tmpP = take(512)
        ytmp = take(768)
        BTr, BTi, CTr, CTi = (v3(take(512), NU) for _ in range(4))
        cT = v3(regC, KC)
        hf = cT
        ucv = v3(regU, KC)
        gsT = ucv[:, :, 0:T]
        uT = v3(regUT, NU)
        cosT, sinT = v3(regTab[:, 0:2048], NST), v3(regTab[:, 2048:4096], NST)
        zr = v3(regZ[:, 0:1024], 2)
        zi = v3(regZ[:, 1024:2048], 2)
        sr, si = regS[:, 0:512], regS[:, 512:1024]
        braw = [v3(regS[:, 256 * i:256 * i + 256], NST) for i in range(2)]
        craw = [v3(regS[:, 512 + 256 * i:768 + 256 * i], NU) for i in range(2)]
        tgF, sgF, hbF = v3(regZ[:, 0:1024], 2), v3(regZ[:, 1024:2048], 2), v3(regUT, 2)
        htok = v3(regU[:, 0:2048], TH)
        acc = v3(regTab[:, 0:2048], TH)
        gfin = regTab[:, 2048:3072]
        tgM, sgM, hhM = regZ[:, 0:512], regZ[:, 512:1024], regZ[:, 1024:1536]
        PM, PT = v3(regZ[:, 1536:1792], TH), regZ[:, 1792:2048]
        ysc = regS
        fin = v3(regC, TH)
        xin = v3(regZ, TH)

        pv = sb("pv", [P, L, PV_N])
        pvh = sb("pvh", [P, L, 16])
        ident = sb("ident", [P, P])
        tri = sb("tri", [P, P])
        onesM = sb("ones", [P, P])
        iota = sb("iota", [P, P])
        par = sb("par", [P, 2])
        pid = sb("pid", [P, 1], I32)
        KL = L * NST
        mag = sb("mag", [P, KL])
        pwr = sb("pwr", [P, 8, KL])
        pwi = sb("pwi", [P, 8, KL])
        cfr = sb("cfr", [P, KL])
        cfi = sb("cfi", [P, KL])
        rw = sb("rw", [P, KC, E])
        nst = sb("nst", [P, 16])
        moe = sb("moe", [P, 64 + 16 * 8])
        rkI = v3(sb("rki", [P, 2 * 12])[:, :], 2)
        gI = v3(sb("gi", [P, 2 * 12])[:, :], 2)
        meta = sb("meta", [P, 4], I32)
        gcur = sb("gcur", [P, 2])
        gslot = sb("gslot", [P, 1])
        zb = sb("zb", [P, 12])

        ps = ctx.enter_context(nc.psum_tensor("ps", [P, 8, 512], F32))

        raw_full = [sem(f"raw_full{i}") for i in range(RAW)]
        hi_ready, lo_ready, unit_used = sem("hi_ready"), sem("lo_ready"), sem("unit_used")
        x_in, par_in, bc_in, out_done = sem("x_in"), sem("par_in"), sem("bc_in"), sem("out_done")
        late_in, zero_ready = sem("late_in"), sem("zero_ready")
        phase_ready, tap_ready, sq_sum, v_half = sem("phase_ready"), sem("tap_ready"), sem("sq_sum"), sem("v_half")
        consts = sem("consts")
        pool_chain, dve_chain, act_chain = sem("pool_chain"), sem("dve_chain"), sem("act_chain")
        ldt_ready = sem("ldt_ready")
        xt_ps, pv_ps, pv_ready, x_copied = sem("xt_ps"), sem("pv_ps"), sem("pv_ready"), sem("x_copied")
        bprep, cprep, bt_ps, ct_ps, bct_ready = (
            sem(n) for n in ("bprep", "cprep", "bt_ps", "ct_ps", "bct_ready"))
        sq_ready, stat_ps, diag_ready, bc_ps, hf_ready, hh_ready, hl_ready = (
            sem(n) for n in ("sq_ready", "stat_ps", "diag_ready", "bc_ps", "hf_ready", "hh_ready", "hl_ready"))
        free_act, free_dve = sem("free_act"), sem("free_dve")
        gate_ready, ph_ready, pl_ready = sem("gate_ready"), sem("ph_ready"), sem("pl_ready")
        tab_ready, bu_ps, rot_done, z_ready, s_ready, y_ps, yd_done, gin_ready, gact_ready, gelu_done = (
            sem(n) for n in ("tab_ready", "bu_ps", "rot_done", "z_ready", "s_ready", "y_ps", "yd_done",
                             "gin_ready", "gact_ready", "gelu_done"))
        yh_ready, yl_ready, gg_done, m_ready, mh_ready, ml_ready = (
            sem(n) for n in ("yh_ready", "yl_ready", "gg_done", "m_ready", "mh_ready", "ml_ready"))
        f_tanh, f_silu, f_hid, f_hi, f_lo, f_out = (
            sem(n) for n in ("f_tanh", "f_silu", "f_hid", "f_hi", "f_lo", "f_out"))
        r_logit, r_diff, r_tanh, r_sel, r_rank, r_meta, ht_ps, ht_ready, xa_ps, acc_init = (
            sem(n) for n in ("r_logit", "r_diff", "r_tanh", "r_sel", "r_rank", "r_meta", "ht_ps",
                             "ht_ready", "xa_ps", "acc_init"))
        e_sel, e_pt_ps, e_pt, e_xg_ps, e_xgh, e_xgl = (
            sem(n) for n in ("e_sel", "e_pt_ps", "e_pt", "e_xg_ps", "e_xgh", "e_xgl"))
        e_tanh, e_silu, e_hid, e_t_ps, e_thi, e_tlo, e_y, e_comb, e_acc = (
            sem(n) for n in ("e_tanh", "e_silu", "e_hid", "e_t_ps", "e_thi", "e_tlo", "e_y", "e_comb", "e_acc"))
        fin_sq, fin_ready = sem("fin_sq"), sem("fin_ready")

        def psum_free(l, s):
            if KINDS[s] in BY_ACT:
                return free_act, l * sum(k in BY_ACT for k in KINDS) + sum(k in BY_ACT for k in KINDS[:s + 1])
            return free_dve, (l * sum(k not in BY_ACT for k in KINDS)
                              + sum(k not in BY_ACT for k in KINDS[:s + 1]))

        def wait_for(eng, pair):
            eng.wait_ge(pair[0], pair[1])

        def half_unit(n0, rounds):
            return n0 if rounds is None else rounds * RAW + n0

        def split_hi(act, n0, rounds=None):
            slot, n = n0 % RAW, half_unit(n0, rounds)
            fills = 16 * (n0 // RAW + 1)
            act.wait_ge(raw_full[slot], fills if rounds is None else rounds * 16 + fills)
            if n0 >= SPL:
                act.wait_ge(unit_used, n - (SPL - 1))
            act.activation(whi[:, slot % SPL, :], raw[:, slot, :], ACT.Copy).then_inc(hi_ready, 1)

        def split_lo(dve, n0, rounds=None):
            slot, n = n0 % RAW, half_unit(n0, rounds)
            dve.wait_ge(hi_ready, n + 1)
            dve.tensor_tensor(wlo[:, slot % SPL, :], raw[:, slot, :],
                              whi[:, slot % SPL, :].bitcast(F32), ALU.subtract).then_inc(lo_ready, 1)

        def load(sp, n0, rounds, src, pattern, k):
            slot, n = n0 % RAW, half_unit(n0, rounds)
            if n0 >= RAW:
                sp.wait_ge(lo_ready, n - (RAW - 1))
            sp.dma_start(raw[:, slot, :].rearrange("p (k n) -> p k n", k=k),
                         src.rearrange(pattern, p=P)).then_inc(raw_full[slot], 16)

        vst = v3(regU[:, 0:256], 2)

        def parameter_rows(eng, l):
            rows = [(PV_B, b_in[l], 44), (PV_NM, norm_mix[l], KC), (PV_NF, norm_ffn[l], KC), (PV_D, ssm_d[l], NU)]
            eng.dma_start(ytmp[0:NST, 2 * l:2 * l + 2], ssm_log_dt[l].rearrange("(r g) -> r g", g=2)).then_inc(par_in, 16)
            for r0, src in ((PV_AR, ssm_a_re), (PV_AI, ssm_a_im)):
                eng.dma_start(vst[r0:r0 + NST, l, :],
                              src[l].rearrange("(r g) n -> r (g n)", g=2)).then_inc(par_in, 16)
            for r0, src, k in rows:
                eng.dma_start(vst[r0:r0 + k, l, :], src.rearrange("(r p) -> r p", p=P)).then_inc(par_in, 16)
            eng.dma_start(vst[PV_CONV:PV_CONV + 24, l, :],
                          conv_w[l].rearrange("w (r p) -> (w r) p", p=P)).then_inc(par_in, 16)

        block = ctx.enter_context(nc.Block())

        @block.sync
        def _(sp):
            parameter_rows(sp, 1)

            def mixer_loads(l):
                for s, (kind, i) in enumerate(zip(KINDS, INDEX)):
                    n = BASE[l] + s
                    if kind in COL0:
                        c0 = COL0[kind] + 256 * i
                        src, k = w_in[l, :, c0:c0 + 256], 8
                    elif kind == "o":
                        src, k = w_conv_out[l, :, 256 * i:256 * i + 256], 8
                    elif kind == "w":
                        src, k = w_o[l, :, 256 * i:256 * i + 256], 8
                    else:
                        c0 = 512 * i + (D if kind == "G" else 0)
                        src, k = w_glu[l, :, c0:c0 + 512], 4
                    load(sp, n, None, src, "(k p) n -> p k n", k)

            def ffn_load(n, rounds, name, b, i):
                if name == "d":
                    src = dense_w_down[0, bass.ds(b * 512 + i * 256, 256), :]
                    load(sp, n, rounds, src, "(k p) n -> p k n", 2)
                else:
                    w = dense_w_gate if name == "g" else dense_w_up
                    load(sp, n, rounds, w[0, :, bass.ds(b * 512 + i * 256, 256)], "(k p) n -> p k n", 8)

            mixer_loads(0)
            n0 = BASE[0] + NSTEP
            for j, (name, i) in enumerate([("g", 0), ("g", 1), ("u", 0), ("u", 1)]):
                ffn_load(n0 + j, None, name, 0, i)
            with sp.Fori(0, NB - 1) as r:
                for j, (name, i) in enumerate(LOOP_STEPS):
                    ffn_load(n0 + 4 + j, r, name, r + (0 if name == "d" else 1), i)
            for i in range(2):
                ffn_load(n0 + ITEM - 2 + i, None, "d", NB - 1, i)

            mixer_loads(1)

            def item_loads(item, e):
                def ld(n, rounds, name, b, i):
                    if name == "d":
                        src = moe_w_down[0, bass.ds(e, 1), bass.ds(b * 512 + i * 256, 256), :]
                        k = 2
                    else:
                        w = moe_w_gate if name == "g" else moe_w_up
                        src = w[0, bass.ds(e, 1), 512 * i:512 * i + 512, bass.ds(b * 512, 512)]
                        k = 4
                    load(sp, n, rounds, src, "a (k p) n -> p (a k) n", k)
                for j, (name, i) in enumerate(HEAD_STEPS):
                    ld(MOE0 + j, item * NB, name, 0, i)
                with sp.Fori(0, NB - 1) as r:
                    for j, (name, i) in enumerate(LOOP_STEPS):
                        ld(MOE0 + 4 + j, item * NB + r, name, r + (0 if name == "d" else 1), i)
                for i in range(2):
                    ld(MOE0 + ITEM - 2 + i, item * NB, "d", NB - 1, i)

            with sp.Fori(0, E) as e:
                item_loads(e, e)
            sp.wait_ge(r_meta, 1)
            n_over = sp.value_load(meta[0:1, 0:1], min_val=0, max_val=3)
            with sp.If(n_over > 0):
                with sp.Fori(0, n_over) as r:
                    e = sp.value_load(meta[0:1, bass.ds(r + 1, 1)], min_val=0, max_val=E - 1)
                    item_loads(r + E, e)
            for j in range(2):
                slot = (MOE0 + j) % RAW
                sp.wait_ge(lo_ready, n_over * ITEM + (MOE0 + E * ITEM + j - (RAW - 1)))
                sp.dma_start(raw[:, slot, 0:16], w_o[0, 0:P, 0:16]).then_inc(raw_full[slot], 16)

            for h in range(TH):
                sp.wait_ge(fin_ready, h + 1)
                sp.dma_start(out[0, h * P:h * P + P, :], fin[:, h, :]).then_inc(out_done, 16)
            sp.wait_ge(out_done, 16 * TH)

        @block.gpsimd
        def _(pool):
            n_chain = [0]

            def link(ins):
                n_chain[0] += 1
                ins.then_inc(pool_chain, 1)
                pool.wait_ge(pool_chain, n_chain[0])

            def mark(ins):
                n_chain[0] += 1
                ins.then_inc(pool_chain, 1)

            pool.dma_start(xin, x[0].rearrange("(h p) d -> p h d", p=P)).then_inc(x_in, 16)
            link(pool.memset(ident[:, :], 0.0))
            pool.affine_select(out=ident[:, :], in_=ident[:, :], compare_op=ALU.not_equal, fill=1.0,
                               base=0, pattern=[[-1, P]], channel_multiplier=1).then_inc(consts, 1)
            pool.memset(onesM[:, :], 1.0).then_inc(consts, 1)
            link(pool.memset(tri[:, :], 1.0))
            pool.affine_select(out=tri[:, :], in_=tri[:, :], compare_op=ALU.is_gt, fill=0.0,
                               base=0, pattern=[[1, P]], channel_multiplier=-1).then_inc(consts, 1)
            pool.iota(iota[:, :], pattern=[[1, P]], base=0, channel_multiplier=0,
                      allow_small_or_imprecise_dtypes=True).then_inc(consts, 1)
            pool.iota(pid[:, :], pattern=[[0, 1]], base=0, channel_multiplier=1).then_inc(consts, 1)

            def power(l, k):
                pr, pi = (w[:, k - 1, l * NST:(l + 1) * NST] for w in (pwr, pwi))
                er, ei = (w[:, k, l * NST:(l + 1) * NST] for w in (pwr, pwi))
                a, b, c, f, g = (tmpP[:, NST * i:NST * (i + 1)] for i in range(5))
                mark(pool.tensor_tensor(a, pr, pr, ALU.mult))
                mark(pool.tensor_tensor(b, pi, pi, ALU.mult))
                link(pool.tensor_tensor(c, pr, pi, ALU.mult))
                mark(pool.tensor_tensor(er, a, b, ALU.subtract))
                link(pool.tensor_tensor(f, a, b, ALU.add))
                mark(pool.tensor_scalar(g, f, -2.0, 4.0, ALU.mult, ALU.add))
                link(pool.tensor_scalar(f, f, -1.0, 2.0, ALU.mult, ALU.add))
                mark(pool.tensor_tensor(ei, c, g, ALU.mult))
                link(pool.tensor_tensor(er, er, f, ALU.mult))

            def double(l, k, m0, m1):
                w = 1 << k
                m = min(m1 - m0, 256 // w)
                for t0 in range(m0, m1, m):
                    ts = slice(t0, t0 + m)
                    er = pwr[:, k, l * NST + t0:l * NST + t0 + m].unsqueeze(2).to_broadcast([P, m, w])
                    ei = pwi[:, k, l * NST + t0:l * NST + t0 + m].unsqueeze(2).to_broadcast([P, m, w])
                    ta, tb = (tmpP[:, 256 * i:256 * i + m * w].rearrange("p (a n) -> p a n", a=m) for i in range(2))
                    c0, s0 = cosT[:, ts, 0:w], sinT[:, ts, 0:w]
                    c1, s1 = cosT[:, ts, w:2 * w], sinT[:, ts, w:2 * w]
                    mark(pool.tensor_tensor(c1, c0, er, ALU.mult))
                    mark(pool.tensor_tensor(s1, c0, ei, ALU.mult))
                    mark(pool.tensor_tensor(ta, s0, ei, ALU.mult))
                    link(pool.tensor_tensor(tb, s0, er, ALU.mult))
                    mark(pool.tensor_tensor(c1, c1, ta, ALU.subtract))
                    link(pool.tensor_tensor(s1, s1, tb, ALU.add))

            def norm_sums(v):
                for i in range(1, SUMMED[v] // 2):
                    pool.wait_ge(sq_ready, 4 * v + i + 1)
                    ins = pool.tensor_tensor(cT[:, 0:2, :], cT[:, 0:2, :], cT[:, 2 * i:2 * i + 2, :], ALU.add)
                    if i < SUMMED[v] // 2 - 1:
                        link(ins)
                ins.then_inc(sq_sum, 1)

            norm_sums(0)
            for n in range(2):
                pool.wait_ge(hi_ready, n + 1)
                pool.tensor_tensor(wlo[:, n, :], raw[:, n, :], whi[:, n, :].bitcast(F32), ALU.subtract).then_inc(lo_ready, 1)

            pool.wait_ge(phase_ready, 1)
            for l in range(L):
                if l:
                    pool.wait_ge(rot_done, 8 * l)
                link(pool.memset(cosT[:, :, 0:1], 1.0))
                link(pool.memset(sinT[:, :, 0:1], 0.0))
                NH = NST // 2
                for k in range(7):
                    if k > 0:
                        power(l, k)
                    if k < 4:
                        double(l, k, 0, NST)
                    else:
                        double(l, k, 0, NH)
                power(l, 7)
                pool.nop().then_inc(tab_ready, 1)
                rest = [[(4, NH, NST)], [(5, NH, NST)], [(6, NH, NH + 4)], [(6, NH + 4, NST)]]
                double(l, *rest[0][0])
                if l:
                    for (piece,) in rest[1:]:
                        double(l, *piece)
                    pool.nop().then_inc(tab_ready, 1)
                    norm_sums(2 * l)
                for q in range(8):
                    m0, m1 = PAIR[q]
                    buf = q % 2
                    C = cosT[:, m0:m1 + 1:4, :].unsqueeze(2).to_broadcast([P, 2, 2, H])
                    S = sinT[:, m0:m1 + 1:4, :].unsqueeze(2).to_broadcast([P, 2, 2, H])

                    def q4(ap):
                        return ap.rearrange("p (a b n) -> p a b n", a=2, b=2)
                    pool.wait_ge(z_ready, 8 * l + q + 1)
                    if q == 0:
                        pool.wait_ge(bct_ready, l + 1)
                    else:
                        pool.wait_ge(y_ps, 8 * l + q)
                    pool.tensor_tensor(q4(sr), C, q4(zr[:, buf, :]), ALU.mult).then_inc(pool_chain, 1)
                    pool.tensor_tensor(q4(si), S, q4(zr[:, buf, :]), ALU.mult).then_inc(pool_chain, 1)
                    n_chain[0] += 2
                    link(pool.tensor_tensor(q4(tmpP), S, q4(zi[:, buf, :]), ALU.mult))
                    link(pool.tensor_tensor(q4(sr), q4(sr), q4(tmpP), ALU.subtract))
                    link(pool.tensor_tensor(q4(tmpP), C, q4(zi[:, buf, :]), ALU.mult))
                    pool.tensor_tensor(q4(si), q4(si), q4(tmpP), ALU.add).then_inc(s_ready, 1)
                    pool.wait_ge(s_ready, 8 * l + q + 1)
                    if l == 0 and q < 3:
                        double(l, *rest[q + 1][0])
                        if q == 2:
                            pool.nop().then_inc(tab_ready, 1)
                if l + 1 < L:
                    pool.wait_ge(y_ps, 8 * (l + 1))
                    for i, (w, c) in enumerate(((ssm_b_re, ssm_c_re), (ssm_b_im, ssm_c_im))):
                        pool.dma_start(braw[i], w[l + 1].rearrange("(m g) n c -> (g n) m c", g=2)).then_inc(late_in, 16)
                        pool.dma_start(craw[i], c[l + 1].rearrange("(j g) c n -> (g c) j n", j=NU)).then_inc(late_in, 16)
                if l + 1 == L:
                    pool.wait_ge(y_ps, 8 * L)
                    pool.dma_start(gfin, norm_final.rearrange("(a n) -> a n", a=1).to_broadcast([P, D])).then_inc(late_in, 16)
                for i in range(2):
                    pool.wait_ge(gate_ready, 10 * l + 8 + i + 1)
                    zg = v3((zr if i == 0 else zi).rearrange("p a n -> p (a n)"), 4)
                    pool.tensor_tensor(gsT[:, 4 * i:4 * i + 4, :], gsT[:, 4 * i:4 * i + 4, :], zg, ALU.mult).then_inc(gg_done, 1)
                for j in range(2):
                    pool.wait_ge(mh_ready, 4 * l + j + 1)
                    pool.tensor_tensor(pL[:, 2 * j:2 * j + 2, :], gsT[:, 2 * j:2 * j + 2, :],
                                       pH[:, 2 * j:2 * j + 2, :].bitcast(F32), ALU.subtract).then_inc(ml_ready, 1)
                norm_sums(2 * l + 1)
            pool.wait_ge(yl_ready, L)
            pool.memset(zeroR.bitcast(F32), 0.0).then_inc(zero_ready, 1)

        @block.scalar
        def _(act):
            n_chain = [0]

            def link(ins):
                n_chain[0] += 1
                ins.then_inc(act_chain, 1)
                act.wait_ge(act_chain, n_chain[0])

            parameter_rows(act, 0)
            act.wait_ge(consts, 5)
            link(act.activation(gslot[:, :], ident[:, 0:1], ACT.Copy))

            def norm_squares(v):
                for i in range(4):
                    if v == 0:
                        act.wait_ge(x_copied, i + 1)
                    elif v == 2:
                        act.wait_ge(f_out, i + 1)
                    else:
                        wait_for(act, psum_free(v // 2, AT["w", i]))
                    act.activation(cT[:, 2 * i:2 * i + 2, :], xT[:, 2 * i:2 * i + 2, :], ACT.Square).then_inc(sq_ready, 1)

            def norm_hi(v):
                for i in range(4):
                    act.wait_ge(hf_ready, 4 * v + i + 1)
                    act.activation(hH[:, 2 * i:2 * i + 2, :], hf[:, 2 * i:2 * i + 2, :], ACT.Copy).then_inc(hh_ready, 1)

            def mixer(l):
                base = BASE[l]
                g0 = l * 10

                def early(s):
                    kind, i = KINDS[s], INDEX[s]
                    if kind not in BY_ACT:
                        return
                    b = bank_of(s)
                    if kind == "G":
                        b0 = (s % 2) * 2
                        act.wait_ge(unit_used, base + s + 1)
                        zg = (zr if i == 0 else zi).rearrange("p a n -> p (a n)")
                        ins = act.activation(zg, ps[:, b0:b0 + 2, :].rearrange("p a n -> p (a n)"), ACT.Tanh, scale=0.5)
                        ins.then_inc(free_act, 1)
                        wait_for(act, psum_free(l, s))
                        act.activation(zg, zg, ACT.Copy, scale=0.5, bias=0.5).then_inc(gate_ready, 1)
                        return
                    act.wait_ge(unit_used, base + s + 1)
                    if kind == "gc":
                        wait_for(act, psum_free(l, AT["b", i]))
                    if kind == "gs":
                        act.wait_ge(pl_ready, 4 * l + i + 1)
                    for j in range(2):
                        t = 2 * i + j
                        src = ps[:, b, 256 * j:256 * j + 256]
                        col = COL0[kind] // P + t
                        if kind in ("u", "c"):
                            dst = uT[:, t, :] if kind == "u" else cT[:, t, :]
                            ins = act.activation(dst, src, ACT.Identity, bias=pv[:, l, PV_B + col:PV_B + col + 1])
                        else:
                            dst = cT[:, t, :] if kind == "gc" else gsT[:, t, :]
                            hcol = t + (0 if kind == "gc" else 8)
                            ins = act.activation(dst, src, ACT.Tanh, scale=0.5, bias=pvh[:, l, hcol:hcol + 1])
                    ins.then_inc(free_act, 1)
                    if kind in ("gc", "gs"):
                        wait_for(act, psum_free(l, s))
                        dst = (cT if kind == "gc" else gsT)[:, 2 * i:2 * i + 2, :]
                        act.activation(dst, dst, ACT.Copy, scale=0.5, bias=0.5).then_inc(gate_ready, 1)

                def late(s):
                    kind, i = KINDS[s], INDEX[s]
                    if kind == "v":
                        wait_for(act, psum_free(l, s))
                        for t in (2 * i, 2 * i + 1):
                            cw = pv[:, l, PV_CONV + t:PV_CONV + t + 1]
                            ins = act.activation(cT[:, t, :], ucv[:, t, 0:T], ACT.Copy, scale=cw)
                        ins.then_inc(tap_ready, 1)
                    if kind == "b":
                        wait_for(act, psum_free(l, s))
                        act.activation(pH[:, 2 * i:2 * i + 2, :], gsT[:, 2 * i:2 * i + 2, :], ACT.Copy).then_inc(ph_ready, 1)
                    if kind == "V":
                        for j in range(2):
                            act.wait_ge(m_ready, 4 * l + 2 * i + j + 1)
                            t = 4 * i + 2 * j
                            act.activation(pH[:, t:t + 2, :], gsT[:, t:t + 2, :], ACT.Copy).then_inc(mh_ready, 1)

                for s in range(NSTEP + 1):
                    if s > 0:
                        early(s - 1)
                    if s == AT["w", 0]:
                        late(s - 1)
                    if s < NSTEP:
                        split_hi(act, base + s + 2)
                    if s > 0 and s != AT["w", 0]:
                        late(s - 1)
                    if s in GELU_AT:
                        gi = GELU_AT.index(s)
                        act.wait_ge(gin_ready, 2 * l + gi + 1)
                        link(act.activation(ytmp[:, 0:512], ytmp[:, 0:512], ACT.Tanh, scale=0.7978845608028654))
                        act.activation(ytmp[:, 0:512], ytmp[:, 0:512], ACT.Copy, scale=0.5, bias=0.5).then_inc(gact_ready, 1)
                    if s == YSPLIT_AT:
                        act.wait_ge(gelu_done, 2 * (l + 1))
                        act.wait_ge(unit_used, base + AT["gs", 3] + 1)
                        act.activation(yH, uT, ACT.Copy).then_inc(yh_ready, 1)

            for i in range(4):
                act.wait_ge(xt_ps, i + 1)
                act.activation(xT[:, 2 * i:2 * i + 2, :].rearrange("p a n -> p (a n)"), ps[:, i, :], ACT.Copy).then_inc(x_copied, 1)
            norm_squares(0)
            split_hi(act, 0)
            split_hi(act, 1)
            for i, (w, c) in enumerate(((ssm_b_re, ssm_c_re), (ssm_b_im, ssm_c_im))):
                act.dma_start(braw[i], w[0].rearrange("(m g) n c -> (g n) m c", g=2)).then_inc(bc_in, 16)
                act.dma_start(craw[i], c[0].rearrange("(j g) c n -> (g c) j n", j=NU)).then_inc(bc_in, 16)
            act.dma_start(rw[:, :, :], router_w[0].rearrange("(k p) e -> p k e", p=P)).then_inc(bc_in, 16)
            act.dma_start(moe[:, 0:E], router_b[0:1, :].to_broadcast([P, E])).then_inc(bc_in, 16)
            norm_hi(0)
            mixer(0)
            norm_squares(1)
            norm_hi(1)

            n0 = NSTEP

            def f_tanh_step(blk, i, n):
                act.wait_ge(unit_used, n + 1)
                act.activation(tgF[:, i, :], ps[:, i, :], ACT.Tanh, scale=0.5).then_inc(f_tanh, 1)

            def f_hi_step(blk, i):
                act.wait_ge(f_hid, blk * 2 + (i + 1))
                act.activation(fH[:, 2 * i:2 * i + 2, :].rearrange("p a n -> p (a n)"), hbF[:, i, :], ACT.Copy).then_inc(f_hi, 1)

            def ffn_slot(blk, r, j):
                n = half_unit(n0 + 4 + j, r)
                if j in (1, 2):
                    f_tanh_step(blk, j - 1, n - 1)
                split_hi(act, n0 + 4 + j + 2, r)
                if j == 0:
                    f_hi_step(blk - 1, 1)
                if j == 5:
                    f_hi_step(blk, 0)

            for j, (name, i) in enumerate(HEAD_STEPS):
                if j in (1, 2):
                    f_tanh_step(0, j - 1, n0 + j - 1)
                split_hi(act, n0 + j + 2)
                if j == 3:
                    f_hi_step(0, 0)
            with act.Fori(0, NB - 1) as r:
                for j in range(6):
                    ffn_slot(r + 1, r, j)
            for j in range(2):
                split_hi(act, n0 + ITEM + j)
                if j == 0:
                    f_hi_step(NB - 1, 1)

            norm_squares(2)
            norm_hi(2)
            mixer(1)
            norm_squares(3)

            for b in range(4):
                act.wait_ge(ht_ps, b + 1)
                act.activation(htok[:, b // 2, 512 * (b % 2):512 * (b % 2) + 512], ps[:, b, :], ACT.Copy).then_inc(ht_ready, 1)
                if b == 1:
                    act.wait_ge(r_diff, 1)
                    act.activation(moe[:, 8:10], moe[:, 10:12], ACT.Tanh, scale=0.5).then_inc(r_tanh, 1)
            act.wait_ge(e_xg_ps, 1)
            act.activation(FR[:, 0:1024], ps[:, 5:7, :].rearrange("p a n -> p (a n)"), ACT.Copy).then_inc(e_xgh, 1)
            for b in range(4):
                act.wait_ge(xa_ps, b + 1)
                bank = XA_BANK[b]
                act.activation(acc[:, b // 2, 512 * (b % 2):512 * (b % 2) + 512], ps[:, bank, :], ACT.Copy).then_inc(acc_init, 1)
            act.wait_ge(r_meta, 1)
            n_over = act.value_load(meta[0:1, 0:1], min_val=0, max_val=3)
            with act.Fori(0, n_over + E) as item:
                m = item * ITEM + MOE0

                def tanh_step(q, n):
                    act.wait_ge(unit_used, n)
                    act.activation(tgM, ps[:, 0, :], ACT.Tanh, scale=0.5).then_inc(e_tanh, 1)

                def thi_step(q):
                    act.wait_ge(e_t_ps, q + 1)
                    act.activation(FR[:, 2048:2560], ps[:, 2, :], ACT.Copy).then_inc(e_thi, 1)

                for j in range(4):
                    if j == 1:
                        act.wait_ge(e_pt_ps, item + 1)
                        act.activation(PT, ps[:, 7, 0:256], ACT.Copy).then_inc(e_pt, 1)
                        act.activation(gslot[:, :], ps[:, 7, 256:257], ACT.Copy).then_inc(e_pt, 1)
                    if j == 2:
                        tanh_step(item * NB, m + 2)
                    split_hi(act, MOE0 + j + 2, item * NB)
                with act.Fori(0, NB - 1) as r:
                    mm = m + r * 6
                    for j in range(6):
                        if j == 1:
                            thi_step(item * NB + r)
                        if j == 2:
                            tanh_step(item * NB + (r + 1), mm + 6)
                        split_hi(act, MOE0 + j + 6, item * NB + r)
                thi_step(item * NB + (NB - 1))
                act.wait_ge(e_xg_ps, item + 2)
                act.activation(FR[:, 0:1024], ps[:, 5:7, :].rearrange("p a n -> p (a n)"), ACT.Copy).then_inc(e_xgh, 1)
                for j in range(2):
                    split_hi(act, MOE0 + ITEM + j, item * NB)
                act.wait_ge(unit_used, m + ITEM)
                act.wait_ge(e_pt, item * 2 + 2)
                act.activation(ysc, ps[:, 3:5, :].rearrange("p a n -> p (a n)"), ACT.Copy,
                               scale=gslot[:, 0:1]).then_inc(e_y, 1)

            for h in range(TH):
                act.wait_ge(e_acc, n_over * 4 + (4 * E - 2 * (TH - 1 - h)))
                act.activation(fin[:, h, :], acc[:, h, :], ACT.Square, accum_out=nst[:, h:h + 1]).then_inc(fin_sq, 1)

        @block.vector
        def _(dve):
            n_chain = [0]

            def link(ins):
                n_chain[0] += 1
                ins.then_inc(dve_chain, 1)
                dve.wait_ge(dve_chain, n_chain[0])

            def mark(ins):
                n_chain[0] += 1
                ins.then_inc(dve_chain, 1)
                return n_chain[0]

            def tt(o, a, b, op):
                return dve.tensor_tensor(o, a, b, op)

            def stt(o, a, s, b, op0, op1):
                return dve.scalar_tensor_tensor(out=o, in0=a, scalar=s, in1=b, op0=op0, op1=op1)

            def ts(o, a, s1, op0, s2=None, op1=None):
                if op1 is None:
                    return dve.tensor_scalar(o, a, s1, None, op0)
                return dve.tensor_scalar(o, a, s1, s2, op0, op1)

            MUL, ADD, SUB = ALU.mult, ALU.add, ALU.subtract

            def inv_sqrt(y, v, a, b):
                mark(ts(b, v, -0.5, MUL))
                link(ts(a.bitcast(I32), v.bitcast(I32), 1, ALU.logical_shift_right))
                link(ts(y.bitcast(I32), a.bitcast(I32), -1.0, MUL, float(0x5F3759DF), ADD))
                for _ in range(3):
                    mark(stt(a[:, 0:1], y[:, 0:1], b[:, 0:1], y[:, 0:1], MUL, MUL))
                    link(stt(a[:, 1:2], y[:, 1:2], b[:, 1:2], y[:, 1:2], MUL, MUL))
                    link(stt(y, a, 1.5, y, ADD, MUL))

            dve.wait_ge(consts, 5)
            dve.wait_ge(par_in, 16 * 8 * L)
            ldx = ytmp[0:NST, 64:64 + L * P].rearrange("p (l g n) -> p (l g) n", l=L, g=2)
            dve.tensor_copy(ldx, ytmp[0:NST, 0:2 * L].unsqueeze(2).to_broadcast([NST, 2 * L, P // 2])).then_inc(ldt_ready, 1)

            dve.wait_ge(pv_ps, 1)
            link(dve.tensor_copy(pv[:, :, :], v3(ps[:, 6, 0:L * PV_N], L)))

            w2 = 2 * KL
            nxt = [1024]

            def t(n=KL):
                nxt[0] += n
                return regU[:, nxt[0] - n:nxt[0]]

            def lay(ap):
                return ap.rearrange("p (l m) -> p l m", l=L)
            ar, ai, dt2, x2, q2, r2, p2, n2, e2 = t(), t(), t(), t(), t(w2), t(w2), t(w2), t(w2), t()
            s1, s2, s3 = t(w2), t(w2), t(w2)
            sn, cs = p2[:, 0:KL], p2[:, KL:w2]

            LOG2E, LN2_HI, LN2_LO = 1.4426950408889634, -0.693359375, 2.12194440e-4
            ek, er_, ep, eb = t(), t(), t(), t()

            def phases():
                mark(dve.tensor_copy(lay(ar), pv[:, :, PV_AR:PV_AR + NST]))
                mark(dve.tensor_copy(lay(ai), pv[:, :, PV_AI:PV_AI + NST]))
                link(dve.tensor_copy(lay(x2), pv[:, :, PV_DT:PV_DT + NST]))
                link(ts(ek, x2, LOG2E, MUL))
                link(ts(ek, ek, -126.0, ALU.max, 127.0, ALU.min))
                link(dve.tensor_copy(eb.bitcast(I32), ek))
                link(dve.tensor_copy(ek, eb.bitcast(I32)))
                mark(ts(eb.bitcast(I32), eb.bitcast(I32), 127.0, ADD))
                link(stt(er_, ek, LN2_HI, x2, MUL, ADD))
                mark(ts(eb.bitcast(I32), eb.bitcast(I32), 23, ALU.logical_shift_left))
                link(stt(er_, ek, LN2_LO, er_, MUL, ADD))
                link(ts(ep, er_, 1.0 / 40320, MUL))
                for c in (5040, 720, 120, 24, 6, 2, 1):
                    link(stt(ep, ep, 1.0 / c, er_, ADD, MUL))
                link(stt(dt2, ep, 1.0, eb, ADD, MUL))
                th, tf, sf = q2, q2[:, 0:KL], q2[:, KL:w2]
                mark(tt(x2, ar, dt2, MUL))
                mark(tt(tf, ai, dt2, MUL))
                link(tt(sf, ai, dt2, MUL))
                mark(ts(ek, x2, LOG2E, MUL))
                mark(ts(s1[:, 0:KL], tf, 0.3183098861837907, MUL))
                link(ts(s1[:, KL:w2], sf, 0.3183098861837907, MUL, -0.5, ADD))
                mark(ts(ek, ek, -126.0, ALU.max, 127.0, ALU.min))
                link(dve.tensor_copy(n2.bitcast(I32), s1))
                mark(dve.tensor_copy(eb.bitcast(I32), ek))
                link(dve.tensor_copy(s1, n2.bitcast(I32)))
                mark(dve.tensor_copy(ek, eb.bitcast(I32)))
                link(ts(s1[:, KL:w2], s1[:, KL:w2], 0.5, ADD))
                mark(stt(er_, ek, LN2_HI, x2, MUL, ADD))
                link(stt(r2, s1, -3.140625, th, MUL, ADD))
                mark(stt(er_, ek, LN2_LO, er_, MUL, ADD))
                link(stt(r2, s1, -9.67502593994140625e-4, r2, MUL, ADD))
                mark(ts(ep, er_, 1.0 / 40320, MUL))
                link(stt(r2, s1, -1.509957990978376432e-7, r2, MUL, ADD))
                mark(stt(ep, ep, 1.0 / 5040, er_, ADD, MUL))
                link(tt(s2, r2, r2, MUL))
                mark(ts(n2.bitcast(I32), n2.bitcast(I32), 1, ALU.bitwise_and))
                link(ts(p2, s2, 1.0 / 6227020800, MUL))
                mark(dve.tensor_copy(s1, n2.bitcast(I32)))
                for c, d in zip((-39916800, 362880, -5040, 120, -6), (720, 120, 24, 6, 2)):
                    mark(stt(ep, ep, 1.0 / d, er_, ADD, MUL))
                    link(stt(p2, p2, 1.0 / c, s2, ADD, MUL))
                mark(ts(s1[:, 0:KL], s1[:, 0:KL], -2.0, MUL, 1.0, ADD))
                mark(ts(s1[:, KL:w2], s1[:, KL:w2], 2.0, MUL, -1.0, ADD))
                mark(stt(ep, ep, 1.0, er_, ADD, MUL))
                mark(ts(eb.bitcast(I32), eb.bitcast(I32), 127.0, ADD))
                link(stt(p2, p2, 1.0, r2, ADD, MUL))
                mark(ts(eb.bitcast(I32), eb.bitcast(I32), 23, ALU.logical_shift_left))
                link(tt(p2, p2, s1, MUL))
                a, b = s2[:, 0:KL], s2[:, KL:w2]
                mark(tt(a, cs, cs, MUL))
                mark(stt(mag[:, :], ep, 1.0, eb, ADD, MUL))
                link(tt(b, sn, sn, MUL))
                link(tt(a, a, b, ADD))
                link(ts(a, a, -0.5, MUL, 1.5, ADD))
                mark(tt(pwr[:, 0, :], cs, a, MUL))
                tt(pwi[:, 0, :], sn, a, MUL).then_inc(phase_ready, 1)

            def coefficients():
                nr, ni, den = e2, r2[:, 0:KL], r2[:, KL:w2]
                a, b, c, d = s1[:, 0:KL], s1[:, KL:w2], s3[:, 0:KL], s3[:, KL:w2]
                mark(tt(nr, mag[:, :], cs, MUL))
                mark(tt(ni, mag[:, :], sn, MUL))
                mark(tt(a, ar, ar, MUL))
                link(tt(b, ai, ai, MUL))
                mark(ts(nr, nr, -1.0, ADD))
                mark(tt(c, ni, ar, MUL))
                link(tt(den, a, b, ADD))
                mark(dve.reciprocal(den, den))
                mark(tt(a, nr, ar, MUL))
                mark(tt(b, ni, ai, MUL))
                link(tt(d, nr, ai, MUL))
                mark(tt(a, a, b, ADD))
                link(tt(c, c, d, SUB))
                mark(tt(cfr[:, :], a, den, MUL))
                link(tt(cfi[:, :], c, den, MUL))

            def prepare_bc(l):
                bd = [v3(regZ[:, 512 * i:512 * i + 512], NST) for i in range(2)]
                cx = [v3(regZ[:, 1024 + 512 * i:1536 + 512 * i], NU) for i in range(2)]
                ls = slice(l * NST, (l + 1) * NST)
                if l == 0:
                    dve.wait_ge(bc_in, 16 * 6)
                else:
                    dve.wait_ge(late_in, 16 * 4)
                kr = cfr[:, ls].unsqueeze(2).to_broadcast([P, NST, CG])
                ki = cfi[:, ls].unsqueeze(2).to_broadcast([P, NST, CG])
                ta, tb = v3(tmpD[:, 0:256], NST), v3(tmpD[:, 256:512], NST)
                link(dve.memset(regZ[:, 0:1024], 0.0))
                for i in range(2):
                    link(tt(ta, kr, braw[i], MUL))
                    link(tt(tb, ki, braw[1 - i], MUL))
                    for g in range(2):
                        rows = slice(64 * g, 64 * g + 64)
                        link(tt(bd[i][rows, :, CG * g:CG * g + CG], ta[rows], tb[rows], SUB if i == 0 else ADD))
                dve.nop().then_inc(bprep, 1)
                for i in range(2):
                    for g in range(2):
                        o = cx[i][:, :, NS * g:NS * g + NS]
                        if i == 0:
                            link(ts(o, craw[i], par[:, g:g + 1], MUL))
                        else:
                            link(ts(o, craw[i], par[:, g:g + 1], MUL, -1.0, MUL))
                dve.nop().then_inc(cprep, 1)

            def finish_bc(l):
                dve.wait_ge(bt_ps, l + 1)
                link(dve.tensor_copy(BTr.rearrange("p a n -> p (a n)"), ps[:, 4, :]))
                link(dve.tensor_copy(BTi.rearrange("p a n -> p (a n)"), ps[:, 5, :]))
                dve.wait_ge(ct_ps, l + 1)
                link(dve.tensor_copy(CTr.rearrange("p a n -> p (a n)"), ps[:, 6, :]))
                dve.tensor_copy(CTi.rearrange("p a n -> p (a n)"), ps[:, 7, :]).then_inc(bct_ready, 1)
                dve.wait_ge(bct_ready, l + 1)

            def norm(v):
                if v == 2:
                    for i in range(4):
                        dve.wait_ge(unit_used, BASE[1])
                        dve.tensor_copy(xT[:, 2 * i:2 * i + 2, :].rearrange("p a n -> p (a n)"), ps[:, 4 + i, :]).then_inc(f_out, 1)
                dve.wait_ge(stat_ps, v + 1)
                link(ts(nst[:, 0:2], ps[:, STAT_BANK[v], 0:2], 1.0 / D, MUL, RMS_EPS, ADD))
                inv_sqrt(nst[:, 2:4], nst[:, 0:2], nst[:, 4:6], nst[:, 6:8])
                for h in range(TH):
                    ts(tmpD[:, P * h:P * h + P], ident[:, :], nst[:, 2 + h:3 + h], MUL).then_inc(diag_ready, 1)
                dve.wait_ge(bc_ps, v + 1)
                pg = PV_NM if v % 2 == 0 else PV_NF

                def scaled(i):
                    for c in (2 * i, 2 * i + 1):
                        ins = stt(hf[:, c, :], xT[:, c, :], pv[:, v // 2, pg + c:pg + c + 1], ps[:, STAT_BANK[v], 256:512], MUL, MUL)
                    ins.then_inc(hf_ready, 1)

                def low(i):
                    dve.wait_ge(hh_ready, 4 * v + i + 1)
                    tt(hL[:, 2 * i:2 * i + 2, :], hf[:, 2 * i:2 * i + 2, :],
                       hH[:, 2 * i:2 * i + 2, :].bitcast(F32), SUB).then_inc(hl_ready, 1)
                scaled(0)
                for i in range(1, 4):
                    scaled(i)
                    if v < 3:
                        low(i - 1)
                if v < 3:
                    low(3)

            def rotate(l, q):
                m0, m1 = PAIR[q]
                buf = q % 2
                C = cosT[:, m0:m1 + 1:4, :].unsqueeze(2).to_broadcast([P, 2, 2, H])
                S = sinT[:, m0:m1 + 1:4, :].unsqueeze(2).to_broadcast([P, 2, 2, H])

                def q4(ap):
                    return ap.rearrange("p (a b n) -> p a b n", a=2, b=2)
                br, bi = q4(ps[:, 4, :]), q4(ps[:, 5, :])
                Zr, Zi, tm = q4(zr[:, buf, :]), q4(zi[:, buf, :]), q4(tmpD)
                dve.wait_ge(bu_ps, 8 * l + q + 1)
                if q % 4 == 0:
                    dve.wait_ge(tab_ready, 2 * l + q // 4 + 1)
                if q >= 2:
                    dve.wait_ge(s_ready, 8 * l + q - 1)
                a = mark(tt(Zr, C, br, MUL))
                b = mark(tt(Zi, C, bi, MUL))
                link(tt(tm, S, bi, MUL))
                link(tt(Zr, Zr, tm, ADD))
                link(tt(tm, S, br, MUL))
                ins = tt(Zi, Zi, tm, SUB)
                ins.then_inc(rot_done, 1)
                dve.wait_ge(rot_done, 8 * l + q + 1)
                mg = [mag[:, l * NST + m:l * NST + m + 1].to_broadcast([P, H]) for m in (m0, m1)]
                last = 0
                for a in range(2):
                    for z in (zr, zi):
                        o = z[:, buf, T * a:T * a + H]
                        last = mark(dve.tensor_tensor_scan(o, mg[a], o, 0.0, MUL, ADD))
                dve.wait_ge(dve_chain, last)
                e_r = pwr[:, 7, l * NST + m0:l * NST + m1 + 1:4]
                e_i = pwi[:, 7, l * NST + m0:l * NST + m1 + 1:4]
                z_r = zr[:, buf, H - 1:H - 1 + T + 1:T]
                z_i = zi[:, buf, H - 1:H - 1 + T + 1:T]
                mark(tt(zb[:, 0:2], e_r, z_r, MUL))
                mark(tt(zb[:, 2:4], e_i, z_i, MUL))
                mark(tt(zb[:, 4:6], e_i, z_r, MUL))
                link(tt(zb[:, 6:8], e_r, z_i, MUL))
                mark(tt(zb[:, 8:10], zb[:, 0:2], zb[:, 2:4], SUB))
                link(tt(zb[:, 10:12], zb[:, 4:6], zb[:, 6:8], ADD))
                for a in range(2):
                    for k, z in enumerate((zr, zi)):
                        o = z[:, buf, T * a + H:T * a + T]
                        ins = dve.tensor_tensor_scan(o, mg[a], o, zb[:, 8 + 2 * k + a:9 + 2 * k + a], MUL, ADD)
                ins.then_inc(z_ready, 1)

            def gelu_in(l, gi):
                dve.wait_ge(y_ps, 8 * l + 4 * (gi + 1))
                for a in range(2):
                    j = 2 * gi + a
                    ins = stt(uT[:, j, :], uT[:, j, :], pv[:, l, PV_D + j:PV_D + j + 1],
                              ps[:, 6, T * a:T * a + T], MUL, ADD)
                    link(ins)
                dve.nop().then_inc(yd_done, 1)
                y2 = uT[:, 2 * gi:2 * gi + 2, :].rearrange("p a n -> p (a n)")
                g = ytmp[:, 0:512]
                link(tt(g, y2, y2, MUL))
                link(ts(g, g, 0.044715, MUL, 1.0, ADD))
                tt(g, g, y2, MUL).then_inc(gin_ready, 1)

            def gelu_out(l, gi):
                y2 = uT[:, 2 * gi:2 * gi + 2, :].rearrange("p a n -> p (a n)")
                dve.wait_ge(gact_ready, 2 * l + gi + 1)
                tt(y2, y2, ytmp[:, 0:512], MUL).then_inc(gelu_done, 1)

            def mixer(l):
                base = BASE[l]

                def early(s):
                    kind, i = KINDS[s], INDEX[s]
                    b = bank_of(s)
                    if kind == "v":
                        dve.wait_ge(unit_used, base + s + 1)
                        wait_for(dve, psum_free(l, AT["c", i]))
                        for j in range(2):
                            t = 2 * i + j
                            col = COL0["v"] // P + t
                            ins = stt(ucv[:, t, 2:2 + T], ps[:, b, T * j:T * j + T],
                                      pv[:, l, PV_B + col:PV_B + col + 1], cT[:, t, :], ADD, MUL)
                            if j == 0:
                                link(ins)
                        ins.then_inc(free_dve, 1)
                    elif kind == "b":
                        dve.wait_ge(unit_used, base + s + 1)
                        for j in range(2):
                            t = 2 * i + j
                            ins = stt(gsT[:, t, :], ps[:, b, T * j:T * j + T],
                                      pv[:, l, PV_B + t:PV_B + t + 1], cT[:, t, :], ADD, MUL)
                        ins.then_inc(free_dve, 1)
                    elif kind == "o":
                        dve.wait_ge(unit_used, base + s + 1)
                        dve.wait_ge(gate_ready, 10 * l + i + 1)
                        g = cT[:, 2 * i:2 * i + 2, :].rearrange("p a n -> p (a n)")
                        tt(g, g, ps[:, b, :], MUL).then_inc(free_dve, 1)
                    elif kind == "V":
                        dve.wait_ge(gg_done, 2 * l + i + 1)
                        wait_for(dve, psum_free(l, AT["o", 3]))
                        b0 = (s % 2) * 2
                        for j in range(2):
                            if j == 0:
                                dve.wait_ge(v_half, 2 * l + i + 1)
                            else:
                                dve.wait_ge(unit_used, base + s + 1)
                            t = 4 * i + 2 * j
                            ins = tt(gsT[:, t:t + 2, :], gsT[:, t:t + 2, :], v3(ps[:, b0 + j, :], 2), MUL)
                            if j == 0:
                                link(ins)
                            else:
                                ins.then_inc(free_dve, 1)
                                wait_for(dve, psum_free(l, s))
                            tt(gsT[:, t:t + 2, :], gsT[:, t:t + 2, :], cT[:, t:t + 2, :], ADD).then_inc(m_ready, 1)
                    elif kind == "w":
                        dve.wait_ge(unit_used, base + s + 1)
                        xx = xT[:, 2 * i:2 * i + 2, :].rearrange("p a n -> p (a n)")
                        tt(xx, xx, ps[:, b, :], ADD).then_inc(free_dve, 1)

                def late(s):
                    kind, i = KINDS[s], INDEX[s]
                    if kind == "v":
                        dve.wait_ge(tap_ready, 4 * l + i + 1)
                        for w in (1, 2):
                            for j in range(2):
                                t = 2 * i + j
                                cw = pv[:, l, PV_CONV + 8 * w + t:PV_CONV + 8 * w + t + 1]
                                k = mark(stt(cT[:, t, :], ucv[:, t, w:w + T], cw, cT[:, t, :], MUL, ADD))
                            dve.wait_ge(dve_chain, k)
                    if kind == "b":
                        dve.wait_ge(ph_ready, 4 * l + i + 1)
                        tt(pL[:, 2 * i:2 * i + 2, :], gsT[:, 2 * i:2 * i + 2, :],
                           pH[:, 2 * i:2 * i + 2, :].bitcast(F32), SUB).then_inc(pl_ready, 1)
                    if kind == "V" and i == 1:
                        dve.wait_ge(ml_ready, 4 * l + 2)
                        for j in range(2):
                            dve.wait_ge(mh_ready, 4 * l + 2 * i + j + 1)
                            t = 4 * i + 2 * j
                            tt(pL[:, t:t + 2, :], gsT[:, t:t + 2, :], pH[:, t:t + 2, :].bitcast(F32), SUB).then_inc(ml_ready, 1)

                for s in range(NSTEP + 1):
                    if s > 0:
                        early(s - 1)
                    if s == BC_AT[l]:
                        finish_bc(l)
                    if s in GELU_AT:
                        gelu_in(l, GELU_AT.index(s))
                    if s == AT["w", 0]:
                        late(s - 1)
                    if s < NSTEP:
                        split_lo(dve, base + s + 2)
                    if s == 0:
                        if l == 0:
                            prepare_bc(0)
                        link(dve.memset(ucv[:, :, 0:2], 0.0))
                    if s > 0 and s != AT["w", 0]:
                        late(s - 1)
                    if s in BU_AT:
                        rotate(l, BU_AT.index(s))
                    if s in GELU_AT:
                        gelu_out(l, GELU_AT.index(s))
                    if s == YSPLIT_AT:
                        dve.wait_ge(yh_ready, l + 1)
                        tt(yL, uT, yH.bitcast(F32), SUB).then_inc(yl_ready, 1)

            phases()
            norm(0)
            coefficients()
            mark(ts(pvh[:, :, :], pv[:, :, PV_B + 28:PV_B + 44], 0.5, MUL))
            link(ts(pid[:, :], pid[:, :], 4, ALU.logical_shift_right, 1, ALU.bitwise_and))
            link(dve.tensor_copy(par[:, 1:2], pid[:, :]))
            link(ts(par[:, 0:1], par[:, 1:2], -1.0, MUL, 1.0, ADD))
            dve.wait_ge(lo_ready, 2)
            mixer(0)
            norm(1)

            n0 = NSTEP

            def f_silu_step(blk, i):
                dve.wait_ge(f_tanh, blk * 2 + (i + 1))
                stt(sgF[:, i, :], tgF[:, i, :], 1.0, ps[:, i, :], ADD, MUL).then_inc(f_silu, 1)

            def f_hid_step(blk, i, n):
                dve.wait_ge(unit_used, n + 1)
                dve.wait_ge(f_silu, blk * 2 + (i + 1))
                stt(hbF[:, i, :], sgF[:, i, :], 0.5, ps[:, 2 + i, :], MUL, MUL).then_inc(f_hid, 1)

            def f_lo_step(blk, i):
                dve.wait_ge(f_hi, blk * 2 + (i + 1))
                tt(fL[:, 2 * i:2 * i + 2, :].rearrange("p a n -> p (a n)"), hbF[:, i, :],
                   fH[:, 2 * i:2 * i + 2, :].rearrange("p a n -> p (a n)").bitcast(F32), SUB).then_inc(f_lo, 1)

            for j in range(4):
                if j in (1, 2):
                    f_silu_step(0, j - 1)
                if j == 3:
                    f_hid_step(0, 0, n0 + 2)
                split_lo(dve, n0 + j + 2)
                if j == 3:
                    f_lo_step(0, 0)
            with dve.Fori(0, NB - 1) as r:
                for j in range(6):
                    n = r * 6 + (n0 + 4 + j)
                    if j == 0:
                        f_hid_step(r, 1, n - 1)
                    if j in (1, 2):
                        f_silu_step(r + 1, j - 1)
                    if j == 5:
                        f_hid_step(r + 1, 0, n - 1)
                    split_lo(dve, n0 + 4 + j + 2, r)
                    if j == 0:
                        f_lo_step(r, 1)
                    if j == 5:
                        f_lo_step(r + 1, 0)
            for j in range(2):
                n = n0 + ITEM - 2 + j
                if j == 0:
                    f_hid_step(NB - 1, 1, n - 1)
                split_lo(dve, n + 2)
                if j == 0:
                    f_lo_step(NB - 1, 1)

            norm(2)
            prepare_bc(1)
            mixer(1)
            norm(3)

            lg = v3(moe[:, 16:32], 2)
            mx = v3(moe[:, 32:48], 2)
            ix = v3(moe[:, 48:64], 2)
            oh0, oh1 = v3(moe[:, 64:80], 2), v3(moe[:, 80:96], 2)
            sel = v3(moe[:, 96:112], 2)
            gt = gI[:, :, 0:E]
            rk = v3(moe[:, 128:144], 2)
            t16 = v3(moe[:, 144:160], 2)
            over, cs = moe[:, 176:184], moe[:, 184:192]
            mark(dve.memset(rkI[:, :, E:12], -1.0))
            mark(dve.memset(gI[:, :, E:12], 0.0))
            dve.wait_ge(r_logit, 1)
            link(tt(lg, v3(ps[:, 6, 0:16], 2), moe[:, 0:E].unsqueeze(1).to_broadcast([P, 2, E]), ADD))
            mark(dve.max(mx[:, 0, :], lg[:, 0, :]))
            link(dve.max(mx[:, 1, :], lg[:, 1, :]))
            tt(moe[:, 10:12], mx[:, :, 0], mx[:, :, 1], SUB).then_inc(r_diff, 1)
            mark(dve.max_index(ix[:, 0, :].bitcast(U32), mx[:, 0, :], lg[:, 0, :]))
            link(dve.max_index(ix[:, 1, :].bitcast(U32), mx[:, 1, :], lg[:, 1, :]))
            link(dve.tensor_copy(t16, ix.bitcast(U32)))
            for h in range(2):
                mark(ts(oh0[:, h, :], iota[:, 0:E], t16[:, h, 0:1], ALU.is_equal))
                ins = ts(oh1[:, h, :], iota[:, 0:E], t16[:, h, 1:2], ALU.is_equal)
                last = mark(ins)
            dve.wait_ge(dve_chain, last)
            tt(sel, oh0, oh1, ADD).then_inc(r_sel, 1)
            dve.wait_ge(r_tanh, 1)
            mark(ts(moe[:, 12:14], moe[:, 8:10], 0.5, MUL, 0.5, ADD))
            link(ts(moe[:, 14:16], moe[:, 8:10], -0.5, MUL, 0.5, ADD))
            mark(ts(gt[:, 0, :], oh0[:, 0, :], moe[:, 12:13], MUL))
            link(ts(gt[:, 1, :], oh0[:, 1, :], moe[:, 13:14], MUL))
            mark(stt(gt[:, 0, :], oh1[:, 0, :], moe[:, 14:15], gt[:, 0, :], MUL, ADD))
            link(stt(gt[:, 1, :], oh1[:, 1, :], moe[:, 15:16], gt[:, 1, :], MUL, ADD))
            dve.wait_ge(r_rank, 1)
            dve.wait_ge(r_sel, 1)
            link(stt(rk, v3(ps[:, 7, 32:48], 2), 1.0, sel, ADD, MUL))
            link(ts(rkI[:, :, 0:E], rk, -1.0, ADD))

            def select_tokens(item):
                for h in range(2):
                    dve.tensor_scalar(PM[:, h, :], iota[:, :], rkI[:, h, item], None, ALU.is_equal).then_inc(e_sel, 1)
                dve.tensor_copy(gcur[:, :].unsqueeze(2), gI[:, :, item]).then_inc(e_sel, 1)

            def xg_lo(count):
                dve.wait_ge(e_xgh, count)
                tt(FR[:, 1024:2048], ps[:, 5:7, :].rearrange("p a n -> p (a n)"), FR[:, 0:1024].bitcast(F32),
                   SUB).then_inc(e_xgl, 1)

            select_tokens(slice(0, 1))

            mj, ids = v3(tmpD[:, 0:24], 3), v3(tmpD[:, 24:48], 3)
            prod, idf = tmpD[:, 48:96].rearrange("p (h j e) -> p h j e", h=2, j=3), tmpD[:, 96:99]
            mj4 = mj.unsqueeze(1).to_broadcast([P, 2, 3, E])
            mark(ts(rk, rk, -float(P), ADD))
            link(ts(over, ps[:, 7, 64:72], float(P), ALU.is_gt))
            link(dve.tensor_tensor_scan(cs, onesM[:, 0:E], over, 0.0, MUL, ADD))
            mark(dve.tensor_copy(meta[:, 0:1], cs[:, E - 1:E]))
            for j in range(3):
                last = mark(ts(mj[:, j, :], cs, float(j + 1), ALU.is_equal))
            dve.wait_ge(dve_chain, last)
            link(tt(mj, mj, over.unsqueeze(1).to_broadcast([P, 3, E]), MUL))
            mark(tt(ids, mj, iota[:, 0:E].unsqueeze(1).to_broadcast([P, 3, E]), MUL))
            link(tt(prod, mj4, rk.unsqueeze(2).to_broadcast([P, 2, 3, E]), MUL))
            mark(dve.reduce_sum(idf, ids, axis=AX.X))
            link(dve.reduce_sum(rkI[:, :, E:E + 3], prod, axis=AX.X))
            mark(dve.tensor_copy(meta[:, 1:4], idf))
            mark(ts(rkI[:, :, E:E + 3], rkI[:, :, E:E + 3], -1.0, ADD))
            link(tt(prod, mj4, gt.unsqueeze(2).to_broadcast([P, 2, 3, E]), MUL))
            link(dve.reduce_sum(gI[:, :, E:E + 3], prod, axis=AX.X))
            dve.nop().then_inc(r_meta, 1)
            xg_lo(1)
            n_over = dve.value_load(meta[0:1, 0:1], min_val=0, max_val=3)
            with dve.Fori(0, n_over + E) as item:
                m = item * ITEM + MOE0

                def silu_step(q):
                    dve.wait_ge(e_tanh, q + 1)
                    stt(sgM, tgM, 1.0, ps[:, 0, :], ADD, MUL).then_inc(e_silu, 1)

                def hid_step(q, n):
                    dve.wait_ge(unit_used, n)
                    dve.wait_ge(e_silu, q + 1)
                    stt(hhM, sgM, 0.5, ps[:, 1, :], MUL, MUL).then_inc(e_hid, 1)

                def tlo_step(q):
                    dve.wait_ge(e_thi, q + 1)
                    tt(FR[:, 2560:3072], ps[:, 2, :], FR[:, 2048:2560].bitcast(F32), SUB).then_inc(e_tlo, 1)

                for j in range(4):
                    if j == 1:
                        dve.wait_ge(e_pt_ps, item + 1)
                        select_tokens(bass.ds(item + 1, 1))
                    if j == 2:
                        silu_step(item * NB)
                    split_lo(dve, MOE0 + j + 2, item * NB)
                with dve.Fori(0, NB - 1) as r:
                    mm = m + r * 6
                    for j in range(6):
                        if j == 0:
                            hid_step(item * NB + r, mm + 4)
                        if j == 1:
                            tlo_step(item * NB + r)
                        if j == 2:
                            silu_step(item * NB + (r + 1))
                        split_lo(dve, MOE0 + j + 6, item * NB + r)
                hid_step(item * NB + (NB - 1), m + (ITEM - 2))
                tlo_step(item * NB + (NB - 1))
                xg_lo(item + 2)
                for j in range(2):
                    split_lo(dve, MOE0 + ITEM + j, item * NB)
                dve.wait_ge(acc_init, 4)
                for k, bank in enumerate(COMB_BANKS):
                    dve.wait_ge(e_comb, item * 4 + (k + 1))
                    dve.wait_ge(e_acc, item * 4)
                    a = acc[:, k // 2, 512 * (k % 2):512 * (k % 2) + 512]
                    tt(a, a, ps[:, bank, :], ADD).then_inc(e_acc, 1)

            dve.wait_ge(fin_sq, TH)
            link(ts(nst[:, 8:10], nst[:, 0:2], 1.0 / D, MUL, RMS_EPS, ADD))
            inv_sqrt(nst[:, 2:4], nst[:, 8:10], nst[:, 4:6], nst[:, 6:8])
            dve.wait_ge(late_in, 16 * 5)
            for h in range(TH):
                stt(fin[:, h, :], acc[:, h, :], nst[:, 2 + h:3 + h], gfin, MUL, MUL).then_inc(fin_ready, 1)

        @block.tensor
        def _(pe):
            pe.wait_ge(consts, 5)
            pe.wait_ge(x_in, 16)
            for i in range(4):
                for c in (2 * i, 2 * i + 1):
                    for h in range(TH):
                        o = (c % 2) * T + h * P
                        ins = pe.transpose(ps[:, i, o:o + P], xin[:, h, c * P:c * P + P], ident[:, :])
                ins.then_inc(xt_ps, 1)
            pe.wait_ge(ldt_ready, 1)
            for l in range(L):
                pe.transpose(ps[:, 6, l * PV_N:l * PV_N + PV_ROWS], vst[0:PV_ROWS, l, :], ident[0:PV_ROWS, 0:PV_ROWS])
                ins = pe.transpose(ps[:, 6, l * PV_N + PV_DT:l * PV_N + PV_N], ytmp[0:NST, 64 + l * P:64 + l * P + P],
                                   ident[0:NST, 0:NST])
            ins.then_inc(pv_ps, 1)

            def three(o, w_h, w_l, x_h, x_l, first, last):
                pe.matmul(o, w_h, x_h, start=first, stop=False, skip_group_check=True)
                pe.matmul(o, w_h, x_l, start=False, stop=False, skip_group_check=True)
                return pe.matmul(o, w_l, x_h, start=False, stop=last, skip_group_check=True)

            def by_chunks(ready, bank, wh, wl, xh, xl):
                for k in range(KC):
                    if k % 2 == 0:
                        pe.wait_ge(ready[0], ready[1] + k // 2 + 1)
                    for j in range(2):
                        cols = slice(P * j, P * j + P)
                        ins = three(ps[:, bank, T * j:T * j + T], wh[:, k, cols], wl[:, k, cols], xh[:, k, :], xl[:, k, :],
                                    k == 0 and j == 0, k == KC - 1)
                return ins

            def norm(v):
                for c in [0, 1] + list(range(SUMMED[v], KC)):
                    if c == 0:
                        pe.wait_ge(sq_sum, v + 1)
                    elif c % 2 == 0:
                        pe.wait_ge(sq_ready, 4 * v + c // 2 + 1)
                    for h in range(TH):
                        ins = pe.matmul(ps[:, STAT_BANK[v], h:h + 1], cT[:, c, h * P:h * P + P], onesM[:, 0:1],
                                        start=(c == 0 and h == 0), stop=(c == KC - 1), skip_group_check=True)
                ins.then_inc(stat_ps, 1)
                for h in range(TH):
                    pe.wait_ge(diag_ready, TH * v + h + 1)
                    ins = pe.matmul(ps[:, STAT_BANK[v], T + h * P:T + h * P + P], onesM[:, :], tmpD[:, h * P:h * P + P],
                                    start=True, stop=True)
                ins.then_inc(bc_ps, 1)

            def prepare_bc(l):
                bd = [regZ[:, 512 * i:512 * i + 512] for i in range(2)]
                cx = [regZ[:, 1024 + 512 * i:1536 + 512 * i] for i in range(2)]
                pe.wait_ge(bprep, l + 1)
                for i in range(2):
                    for j in range(NU):
                        ins = pe.transpose(ps[:, 4 + i, P * j:P * j + P], bd[i][:, P * j:P * j + P], ident[:, :])
                ins.then_inc(bt_ps, 1)
                pe.wait_ge(cprep, l + 1)
                pe.wait_ge(hf_ready, 8 * l + 4)
                for i in range(2):
                    for j in range(NU):
                        ins = pe.transpose(ps[:, 6 + i, P * j:P * j + P], cx[i][:, P * j:P * j + P], ident[:, :])
                ins.then_inc(ct_ps, 1)

            def drive_states(l, q):
                wait_for(pe, psum_free(l, AT["u", 1]))
                pe.wait_ge(bct_ready, l + 1)
                if q > 0:
                    pe.wait_ge(rot_done, 8 * l + q)
                r = 32 * (q % 4)
                for a, m in enumerate(PAIR[q]):
                    for k, w in enumerate((BTr, BTi)):
                        ins = pe.matmul(ps[:, 4 + k, T * a:T * a + T], w[r:r + 32, m // 4, :], uT[r:r + 32, m // 4, :],
                                        start=True, stop=True)
                ins.then_inc(bu_ps, 1)

            def read_states(l, q):
                pe.wait_ge(s_ready, 8 * l + q + 1)
                if q == 4:
                    pe.wait_ge(yd_done, 2 * l + 1)
                r = 32 * (q % 4)
                for a, m in enumerate(PAIR[q]):
                    for k, (w, s) in enumerate(((CTr, sr), (CTi, si))):
                        ins = pe.matmul(ps[r:r + 32, 6, T * a:T * a + T], w[:, m // 4, r:r + 32], s[:, T * a:T * a + T],
                                        start=(k == 0), stop=(k == 1))
                ins.then_inc(y_ps, 1)

            def mixer(l):
                base = BASE[l]
                for s, (kind, i) in enumerate(zip(KINDS, INDEX)):
                    n = base + s
                    if s == BC_AT[l] - 1:
                        prepare_bc(l)
                    if s in BU_AT:
                        drive_states(l, BU_AT.index(s))
                    if s in Y_AT:
                        read_states(l, Y_AT.index(s))
                    pe.wait_ge(lo_ready, n + 1)
                    if s >= 2:
                        wait_for(pe, psum_free(l, s - 2))
                    slot = n % SPL
                    if kind in ("G", "V"):
                        pe.wait_ge(yl_ready, l + 1)
                        wh, wl = v3(whi[:, slot, :], 4), v3(wlo[:, slot, :], 4)
                        tiles = [(ps[:, (s % 2) * 2 + j // 2, T * (j % 2):T * (j % 2) + T], j) for j in range(4)]
                        kc, xh, xl = 4, yH, yL
                    else:
                        wh, wl = v3(whi[:, slot, :], 8), v3(wlo[:, slot, :], 8)
                        tiles = [(ps[:, bank_of(s), T * j:T * j + T], j) for j in range(2)]
                        kc, (xh, xl) = 8, ((hH, hL) if kind in COL0 else (pH, pL))
                    if kind == "o":
                        pe.wait_ge(pl_ready, 4 * (l + 1))
                    if s in (0, AT["w", 0]):
                        ready = (hl_ready, 8 * l) if s == 0 else (ml_ready, 4 * l)
                        ins = by_chunks(ready, bank_of(s), wh, wl, xh, xl)
                    else:
                        for o, j in tiles:
                            for k in range(kc):
                                cols = slice(P * j, P * j + P)
                                ins = three(o, wh[:, k, cols], wl[:, k, cols], xh[:, k, :], xl[:, k, :], k == 0, k == kc - 1)
                            if kind == "V" and j == 1:
                                ins.then_inc(v_half, 1)
                    ins.then_inc(unit_used, 1)

            norm(0)
            mixer(0)
            norm(1)

            n0 = NSTEP

            def up_or_gate(n, slot, bank, first_use=False):
                wh, wl = v3(whi[:, slot % SPL, :], 8), v3(wlo[:, slot % SPL, :], 8)
                pe.wait_ge(lo_ready, n + 1)
                if first_use:
                    by_chunks((hl_ready, 4), bank, wh, wl, hH, hL).then_inc(unit_used, 1)
                    return
                for j in range(2):
                    for k in range(8):
                        cols = slice(P * j, P * j + P)
                        ins = three(ps[:, bank, T * j:T * j + T], wh[:, k, cols], wl[:, k, cols],
                                    hH[:, k, :], hL[:, k, :], k == 0, k == 7)
                ins.then_inc(unit_used, 1)

            def down(n, slot, blk, i, last=False):
                wh, wl = v3(whi[:, slot % SPL, :], 2), v3(wlo[:, slot % SPL, :], 2)
                pe.wait_ge(lo_ready, n + 1)
                pe.wait_ge(f_lo, blk * 2 + (i + 1))
                for j in range(KC):
                    for k in range(2):
                        cols = slice(P * j, P * j + P)
                        ins = three(ps[:, 4 + j // 2, T * (j % 2):T * (j % 2) + T], wh[:, k, cols], wl[:, k, cols],
                                    fH[:, 2 * i + k, :], fL[:, 2 * i + k, :], False, last and k == 1)
                ins.then_inc(unit_used, 1)

            for j, (name, i) in enumerate(HEAD_STEPS):
                n = n0 + j
                up_or_gate(n, n % RAW, j, first_use=(j == 0))
            pe.wait_ge(hf_ready, 8)
            for i in range(4):
                pe.matmul(ps[:, 4 + i, :], ident[:, :], xT[:, 2 * i:2 * i + 2, :], start=True, stop=False, skip_group_check=True)
            with pe.Fori(0, NB - 1) as r:
                for j, (name, i) in enumerate(LOOP_STEPS):
                    n = r * 6 + (n0 + 4 + j)
                    slot = (n0 + 4 + j) % RAW
                    if name == "g":
                        pe.wait_ge(f_silu, r * 2 + (i + 1))
                        up_or_gate(n, slot, i)
                    elif name == "u":
                        pe.wait_ge(f_hid, r * 2 + (i + 1))
                        up_or_gate(n, slot, 2 + i)
                    else:
                        down(n, slot, r, i)
            for i in range(2):
                down(n0 + ITEM - 2 + i, (n0 + ITEM - 2 + i) % RAW, NB - 1, i, last=(i == 1))

            norm(2)
            pe.wait_ge(f_out, 4)
            mixer(1)
            norm(3)

            pe.wait_ge(bc_in, 16 * 6)
            for c in range(KC):
                if c % 2 == 0:
                    pe.wait_ge(hf_ready, 12 + c // 2 + 1)
                for h in range(TH):
                    ins = pe.matmul(ps[:, 6, E * h:E * h + E], hf[:, c, h * P:h * P + P], rw[:, c, :],
                                    start=(c == 0 and h == 0), stop=(c == KC - 1), skip_group_check=True)
            ins.then_inc(r_logit, 1)
            wait_for(pe, psum_free(1, NSTEP - 1))
            for h in range(TH):
                for c in range(KC):
                    ins = pe.transpose(ps[:, 2 * h + c // 4, P * (c % 4):P * (c % 4) + P], hf[:, c, h * P:h * P + P], ident[:, :])
                    if c % 4 == 3:
                        ins.then_inc(ht_ps, 1)
            pe.wait_ge(r_sel, 1)
            sel = v3(moe[:, 96:112], 2)
            pe.matmul(ps[:, 7, 32:40], tri[:, :], sel[:, 0, :], start=True, stop=True)
            pe.matmul(ps[:, 7, 40:48], onesM[:, :], sel[:, 0, :], start=True, stop=False)
            pe.matmul(ps[:, 7, 40:48], tri[:, :], sel[:, 1, :], start=False, stop=True)
            pe.matmul(ps[:, 7, 64:72], onesM[:, :], sel[:, 0, :], start=True, stop=False)
            pe.matmul(ps[:, 7, 64:72], onesM[:, :], sel[:, 1, :], start=False, stop=True).then_inc(r_rank, 1)

            def turn_residual(b):
                h = b // 2
                for c in range(4 * (b % 2), 4 * (b % 2) + 4):
                    ins = pe.transpose(ps[:, XA_BANK[b], P * (c % 4):P * (c % 4) + P], xT[:, c, h * P:h * P + P], ident[:, :])
                ins.then_inc(xa_ps, 1)

            def gather(count):
                pe.wait_ge(e_sel, count * 3)
                for c in range(KC):
                    for h in range(TH):
                        ins = pe.matmul(ps[:, 5 + c // 4, P * (c % 4):P * (c % 4) + P], htok[:, h, c * P:c * P + P],
                                        PM[:, h, :], start=(h == 0), stop=(h == TH - 1))
                ins.then_inc(e_xg_ps, 1)

            turn_residual(0)
            pe.wait_ge(ht_ready, 4)
            gather(1)
            for b in range(1, 4):
                turn_residual(b)
            pe.wait_ge(r_meta, 1)
            n_over = pe.value_load(meta[0:1, 0:1], min_val=0, max_val=3)

            def expert_product(n, slot, bank, i):
                wh, wl = v3(whi[:, slot % SPL, :], 4), v3(wlo[:, slot % SPL, :], 4)
                pe.wait_ge(lo_ready, n + 1)
                for k in range(4):
                    o, c = ps[:, bank, :], 4 * i + k
                    pe.matmul(o, xgH[:, c, :], wh[:, k, :], start=(c == 0), stop=False, skip_group_check=True)
                    pe.matmul(o, xgH[:, c, :], wl[:, k, :], start=False, stop=False, skip_group_check=True)
                    ins = pe.matmul(o, xgL[:, c, :], wh[:, k, :], start=False, stop=(c == KC - 1), skip_group_check=True)
                ins.then_inc(unit_used, 1)

            def expert_down(n, slot, q, i, last=False):
                wh, wl = v3(whi[:, slot % SPL, :], 2), v3(wlo[:, slot % SPL, :], 2)
                pe.wait_ge(lo_ready, n + 1)
                pe.wait_ge(e_tlo, q + 1)
                for k in range(2):
                    for j in range(2):
                        o, c, cols = ps[:, 3 + j, :], 2 * i + k, slice(512 * j, 512 * j + 512)
                        pe.matmul(o, tH[:, c, :], wh[:, k, cols], start=False, stop=False, skip_group_check=True)
                        pe.matmul(o, tH[:, c, :], wl[:, k, cols], start=False, stop=False, skip_group_check=True)
                        ins = pe.matmul(o, tL[:, c, :], wh[:, k, cols], start=False, stop=last and c == 3, skip_group_check=True)
                ins.then_inc(unit_used, 1)

            def turn_hidden(q):
                pe.wait_ge(e_hid, q + 1)
                for c in range(4):
                    ins = pe.transpose(ps[:, 2, P * c:P * c + P], hhM[:, P * c:P * c + P], ident[:, :])
                ins.then_inc(e_t_ps, 1)

            with pe.Fori(0, n_over + E) as item:
                m = item * ITEM + MOE0
                q0 = item * NB
                pe.wait_ge(e_xgl, item + 1)
                for j, (name, i) in enumerate(HEAD_STEPS):
                    if j == 0:
                        pe.wait_ge(e_silu, q0)
                    if j == 2:
                        pe.wait_ge(e_hid, q0)
                        pe.wait_ge(acc_init, 4)
                    expert_product(m + j, (MOE0 + j) % RAW, 0 if name == "g" else 1, i)
                    if j == 0:
                        pe.wait_ge(e_acc, item * 4)
                        for h in range(TH):
                            pe.transpose(ps[:, 7, P * h:P * h + P], PM[:, h, :], ident[:, :])
                        pe.matmul(ps[:, 7, 256:257], PM[:, 0, :], gcur[:, 0:1], start=True, stop=False)
                        pe.matmul(ps[:, 7, 256:257], PM[:, 1, :], gcur[:, 1:2], start=False, stop=True).then_inc(e_pt_ps, 1)
                pe.wait_ge(zero_ready, 1)
                pe.wait_ge(e_y, item)
                for j in range(2):
                    pe.matmul(ps[:, 3 + j, :], zeroR, xgH[:, 0:4, :], start=True, stop=False, skip_group_check=True)
                with pe.Fori(0, NB - 1) as r:
                    mm = m + r * 6
                    q = q0 + r
                    for j, (name, i) in enumerate(LOOP_STEPS):
                        n, slot = mm + (4 + j), (MOE0 + 4 + j) % RAW
                        if j == 0:
                            pe.wait_ge(e_silu, q + 1)
                        if j == 4:
                            pe.wait_ge(e_hid, q + 1)
                        if name == "d":
                            expert_down(n, slot, q, i)
                        else:
                            expert_product(n, slot, 0 if name == "g" else 1, i)
                        if j == 0:
                            turn_hidden(q)
                gather(item + 2)
                turn_hidden(q0 + (NB - 1))
                for i in range(2):
                    expert_down(m + (ITEM - 2 + i), (MOE0 + ITEM - 2 + i) % RAW, q0 + (NB - 1), i, last=(i == 1))
                pe.wait_ge(e_y, item + 1)
                pe.wait_ge(e_pt, item * 2 + 2)
                pe.wait_ge(e_xgl, item + 2)
                for k, bank in enumerate(COMB_BANKS):
                    pe.matmul(ps[:, bank, :], PT[:, P * (k // 2):P * (k // 2) + P], ysc[:, 512 * (k % 2):512 * (k % 2) + 512],
                              start=True, stop=True).then_inc(e_comb, 1)


HEAD_STEPS = [("g", 0), ("g", 1), ("u", 0), ("u", 1)]
LOOP_STEPS = [("g", 0), ("g", 1), ("d", 0), ("d", 1), ("u", 0), ("u", 1)]
COMB_BANKS = (5, 6, 7, 2)


_INS = ["x", "norm_mix", "w_in", "b_in", "conv_w", "w_conv_out", "ssm_a_re", "ssm_a_im", "ssm_log_dt",
        "ssm_b_re", "ssm_b_im", "ssm_c_re", "ssm_c_im", "ssm_d", "w_glu", "w_o", "norm_ffn",
        "dense_w_gate", "dense_w_up", "dense_w_down", "router_w", "router_b",
        "moe_w_gate", "moe_w_up", "moe_w_down", "norm_final"]


def kernel(**inputs):
    import numpy as _np
    import concourse.bacc as _bacc
    from concourse import mybir as _mybir
    from concourse.bass_utils import run_bass_kernel_spmd as _run

    nc = _bacc.Bacc("TRN2", target_bir_lowering=False, num_devices=1)
    arrays, args = {}, []
    for name in _INS:
        a = _np.ascontiguousarray(inputs[name])
        arrays[f"in_{name}"] = a
        args.append(nc.dram_tensor(f"in_{name}", a.shape, _mybir.dt.from_np(a.dtype), kind="ExternalInput").ap())
    shape = inputs["x"].shape
    args.append(nc.dram_tensor("out_0", shape, _mybir.dt.float32, kind="ExternalOutput").ap())
    hybrid_encoder_kernel(nc, *args)
    r = _run(nc, [arrays], core_ids=[0])
    return r.results[0]["out_0"]
```
